# Optimizing a Trainium2 kernel written in Bass

```python
import math
import jax, jax.numpy as jnp
from jax import lax
import numpy as np

D_MODEL = 2048
BATCH = 1
SEQ = 512
DEPTH = 1
DEC_BATCH = 8
DEC_SEQ = 4
PAST_LEN = 4096
PAGE_SIZE = 128

HEAD_DIM = 64
ATT_WIDTH = D_MODEL // 4
ATT_HEADS = ATT_WIDTH // HEAD_DIM
ATT_KV_HEADS = ATT_HEADS // 4
ATT_GROUP = ATT_HEADS // ATT_KV_HEADS
ATT_KV_WIDTH = ATT_KV_HEADS * HEAD_DIM
WINDOW = 128
N_BUCKETS = 32
MAX_DISTANCE = 128
POOL_WIDTH = D_MODEL // 4
POOL_WINDOWS = (2, 4, 8, 16)
POOL_GROUPS = len(POOL_WINDOWS)
POOL_GROUP_DIM = POOL_WIDTH // POOL_GROUPS
POOL_BUF = max(POOL_WINDOWS) - 1
GLA_HEADS = 4
GLA_VALUE_WIDTH = D_MODEL // 2
GLA_KEY_WIDTH = GLA_VALUE_WIDTH // 2
GLA_DK = GLA_KEY_WIDTH // GLA_HEADS
GLA_DV = GLA_VALUE_WIDTH // GLA_HEADS
GLA_GATE_RANK = 16
GLA_GATE_TAU = 16.0
GLA_CHUNK = 32
MIX_WIDTH = ATT_WIDTH + POOL_WIDTH + GLA_VALUE_WIDTH
IN_SPLITS = (ATT_WIDTH, ATT_KV_WIDTH, ATT_KV_WIDTH, POOL_WIDTH,
             GLA_KEY_WIDTH, GLA_KEY_WIDTH, GLA_VALUE_WIDTH, GLA_VALUE_WIDTH)
IN_WIDTH = sum(IN_SPLITS) + GLA_GATE_RANK
D_FF = -(-8 * D_MODEL // (3 * 256)) * 256
N_MOD = 6
EPS = 1e-6

kernel_name = 'hymba_swa_pool_gla_decode_step'

def rmsnorm(x, g):
    xf = x.astype(jnp.float32)
    y = xf * lax.rsqrt(jnp.mean(xf * xf, axis=-1, keepdims=True) + EPS)
    return (y * g.astype(jnp.float32)).astype(x.dtype)

def t5_bucket(dist):
    n = jnp.maximum(dist, 0)
    max_exact = N_BUCKETS // 2
    nf = jnp.maximum(n, max_exact).astype(jnp.float32)
    large = max_exact + (jnp.log(nf / max_exact) / math.log(MAX_DISTANCE / max_exact)
                         * (N_BUCKETS - max_exact)).astype(jnp.int32)
    large = jnp.minimum(large, N_BUCKETS - 1)
    return jnp.where(n < max_exact, n, large)

def sink_attention(q, k, v, dist, valid, rel_bias, sinks):
    f32 = jnp.float32
    logits = jnp.einsum('...qhgd,...khd->...hgqk', q.astype(f32), k.astype(f32)) * (HEAD_DIM ** -0.5)
    bias = rel_bias.astype(f32)[t5_bucket(dist)]
    bias = jnp.moveaxis(bias, -1, 0).reshape(ATT_KV_HEADS, ATT_GROUP, *dist.shape)
    logits = jnp.where(valid, logits + bias, -jnp.inf)
    sink = sinks.astype(f32).reshape(ATT_KV_HEADS, ATT_GROUP, 1, 1)
    m = jnp.maximum(jnp.max(logits, axis=-1, keepdims=True), sink)
    p = jnp.exp(logits - m)
    denom = jnp.sum(p, axis=-1, keepdims=True) + jnp.exp(sink - m)
    return jnp.einsum('...hgqk,...khd->...qhgd', p / denom, v.astype(f32))

def window_attn_prompt(q, k, v, rel_bias, sinks):
    B, T = q.shape[:2]
    nb = T // WINDOW
    qb = q.reshape(B, nb, WINDOW, ATT_KV_HEADS, ATT_GROUP, HEAD_DIM)

    def band(t):
        cur = t.reshape(B, nb, WINDOW, ATT_KV_HEADS, HEAD_DIM)
        prev = jnp.concatenate([jnp.zeros_like(cur[:, :1]), cur[:, :-1]], axis=1)
        return jnp.concatenate([prev, cur], axis=2)

    kb, vb = band(k), band(v)
    r = jnp.arange(WINDOW)
    j = jnp.arange(2 * WINDOW)
    dist = WINDOW + r[:, None] - j[None, :]
    kpos = (jnp.arange(nb)[:, None] - 1) * WINDOW + j[None, :]
    valid = ((dist >= 0) & (dist < WINDOW))[None] & (kpos >= 0)[:, None, :]
    valid = valid[:, None, None]
    o = sink_attention(qb, kb, vb, dist, valid, rel_bias, sinks)
    return o.reshape(B, T, ATT_WIDTH)

def window_attn_sample(q, k, v, k_past, v_past, rel_bias, sinks):
    B, T = q.shape[:2]
    lb = k_past.shape[1]
    kk = jnp.concatenate([k_past.astype(k.dtype), k], axis=1)
    vv = jnp.concatenate([v_past.astype(v.dtype), v], axis=1)
    krel = jnp.arange(-lb, T)
    qrel = jnp.arange(T)
    dist = qrel[:, None] - krel[None, :]
    valid = (dist >= 0) & (dist < WINDOW)
    o = sink_attention(q, kk, vv, dist, valid, rel_bias, sinks)
    return o.reshape(B, T, ATT_WIDTH), kk[:, -lb:], vv[:, -lb:]

def pool_mixer(u, buf, pos0, w_pool, scale):
    B, T, _ = u.shape
    L = POOL_BUF
    ext = jnp.concatenate([buf.astype(u.dtype), u], axis=1).astype(jnp.float32)
    cs = jnp.cumsum(ext, axis=1)
    cs = jnp.concatenate([jnp.zeros_like(cs[:, :1]), cs], axis=1)
    pos = pos0 + jnp.arange(T)
    groups = []
    for gi, w in enumerate(POOL_WINDOWS):
        sl = slice(gi * POOL_GROUP_DIM, (gi + 1) * POOL_GROUP_DIM)
        s = cs[:, L + 1:L + 1 + T, sl] - cs[:, L + 1 - w:L + 1 - w + T, sl]
        cnt = jnp.minimum(w, pos + 1).astype(jnp.float32)
        groups.append(s / cnt[None, :, None])
    pooled = jnp.concatenate(groups, axis=-1)
    d = (pooled - u.astype(jnp.float32)).reshape(B, T, POOL_GROUPS, POOL_GROUP_DIM)
    y = jnp.einsum('btgc,gcd->btgd', d, w_pool.astype(jnp.float32)).reshape(B, T, POOL_WIDTH)
    return y * scale.astype(jnp.float32), ext[:, -L:].astype(u.dtype)

def gla_mixer(q, k, v, log_a, S0):
    B, T, H, dk = q.shape
    dv = v.shape[-1]
    C = GLA_CHUNK
    n = -(-T // C)
    pad = n * C - T

    def prep(t):
        t = jnp.pad(t.astype(jnp.float32), ((0, 0), (0, pad), (0, 0), (0, 0)))
        return t.reshape(B, n, C, H, t.shape[-1]).transpose(1, 0, 3, 2, 4)

    q, k, v, g = prep(q), prep(k), prep(v), prep(log_a)
    b = jnp.cumsum(g, axis=3)
    qd = q * jnp.exp(b) * (dk ** -0.5)
    kd = k * jnp.exp(-b)
    b_last = b[:, :, :, -1:]
    kdec = k * jnp.exp(b_last - b)
    mask = jnp.tril(jnp.ones((C, C), dtype=bool))
    A = jnp.where(mask, jnp.einsum('nbhtd,nbhsd->nbhts', qd, kd), 0.0)
    o_intra = jnp.einsum('nbhts,nbhse->nbhte', A, v)

    def step(S, xs):
        qd_i, kdec_i, v_i, bl_i = xs
        o_i = jnp.einsum('bhtd,bhde->bhte', qd_i, S)
        S = jnp.exp(bl_i)[:, :, 0, :, None] * S + jnp.einsum('bhsd,bhse->bhde', kdec_i, v_i)
        return S, o_i

    S, o_inter = lax.scan(step, S0.astype(jnp.float32), (qd, kdec, v, b_last))
    o = (o_intra + o_inter).transpose(1, 0, 3, 2, 4).reshape(B, n * C, H, dv)[:, :T]
    return o, S

def run_trunk(x, c, win_k, win_v, pool_buf, gla_state, pos0,
              w_ada, b_ada, g_mix, g_ffn, w_in, w_out, rel_bias, sinks, w_pool, pool_scale,
              w_a2, b_a2, g_gla, w_gu, w_down, g_final):
    B, T, _ = x.shape
    split_idx = [int(s) for s in np.cumsum(IN_SPLITS)]
    lb = min(WINDOW, PAST_LEN)
    new_k, new_v, new_pool, new_gla = [], [], [], []
    for l in range(DEPTH):
        mod = jnp.dot(jax.nn.silu(c), w_ada[l]) + b_ada[l]
        sh1, sc1, g1, sh2, sc2, g2 = jnp.split(mod[:, None, :], N_MOD, axis=-1)
        h = rmsnorm(x, g_mix[l]) * (1 + sc1) + sh1
        z = jnp.dot(h, w_in[l])
        zq, zk, zv, zu, gq, gk, gv, gg, ga = jnp.split(z, split_idx, axis=-1)

        q = zq.reshape(B, T, ATT_KV_HEADS, ATT_GROUP, HEAD_DIM)
        k = zk.reshape(B, T, ATT_KV_HEADS, HEAD_DIM)
        v = zv.reshape(B, T, ATT_KV_HEADS, HEAD_DIM)
        if win_k is None:
            o_a = window_attn_prompt(q, k, v, rel_bias, sinks[l])
            nk, nv = k[:, -lb:], v[:, -lb:]
        else:
            o_a, nk, nv = window_attn_sample(q, k, v, win_k[l], win_v[l], rel_bias, sinks[l])

        buf = jnp.zeros((B, POOL_BUF, POOL_WIDTH), x.dtype) if pool_buf is None else pool_buf[l]
        o_b, nbuf = pool_mixer(zu, buf, pos0, w_pool[l], pool_scale[l])

        log_a = jax.nn.log_sigmoid(jnp.dot(ga, w_a2[l]).astype(jnp.float32)
                                   + b_a2[l].astype(jnp.float32)) / GLA_GATE_TAU
        S0 = (jnp.zeros((B, GLA_HEADS, GLA_DK, GLA_DV), jnp.float32)
              if gla_state is None else gla_state[l])
        o_c, S = gla_mixer(gq.reshape(B, T, GLA_HEADS, GLA_DK), gk.reshape(B, T, GLA_HEADS, GLA_DK),
                           gv.reshape(B, T, GLA_HEADS, GLA_DV), log_a.reshape(B, T, GLA_HEADS, GLA_DK), S0)
        o_c = rmsnorm(o_c, g_gla[l].reshape(GLA_HEADS, GLA_DV)) * jax.nn.silu(
            gg.reshape(B, T, GLA_HEADS, GLA_DV).astype(jnp.float32))
        o_c = o_c.reshape(B, T, GLA_VALUE_WIDTH)

        mix = jnp.concatenate([o_a, o_b, o_c], axis=-1).astype(x.dtype)
        x = x + g1 * jnp.dot(mix, w_out[l])

        h2 = rmsnorm(x, g_ffn[l]) * (1 + sc2) + sh2
        gate, up = jnp.split(jnp.dot(h2, w_gu[l]), 2, axis=-1)
        x = x + g2 * jnp.dot(jax.nn.silu(gate) * up, w_down[l])

        new_k.append(nk)
        new_v.append(nv)
        new_pool.append(nbuf)
        new_gla.append(S.astype(jnp.float32))
    y = rmsnorm(x, g_final)
    return y, jnp.stack(new_k), jnp.stack(new_v), jnp.stack(new_pool), jnp.stack(new_gla)

def setup_inputs(seed: int = 0) -> dict:
    key = jax.random.key(seed)
    ks = jax.random.split(key, 24)
    f32 = jnp.float32

    def nrm(k, shape, s=1.0):
        return jax.random.normal(k, shape, f32) * s

    lb = min(WINDOW, PAST_LEN)
    return {
        'x_prompt': nrm(ks[0], (BATCH, SEQ, D_MODEL)),
        'x_sample': nrm(ks[1], (DEC_BATCH, DEC_SEQ, D_MODEL)),
        'cache_win_k': nrm(ks[2], (DEPTH, DEC_BATCH, lb, ATT_KV_HEADS, HEAD_DIM)),
        'cache_win_v': nrm(ks[3], (DEPTH, DEC_BATCH, lb, ATT_KV_HEADS, HEAD_DIM)),
        'state_pool': nrm(ks[4], (DEPTH, DEC_BATCH, POOL_BUF, POOL_WIDTH)),
        'state_gla': nrm(ks[5], (DEPTH, DEC_BATCH, GLA_HEADS, GLA_DK, GLA_DV), 4.0),
        'c_prompt': nrm(ks[6], (BATCH, D_MODEL)),
        'c_sample': nrm(ks[7], (DEC_BATCH, D_MODEL)),
        'w_ada': nrm(ks[8], (DEPTH, D_MODEL, N_MOD * D_MODEL), 0.5 * D_MODEL ** -0.5),
        'b_ada': nrm(ks[9], (DEPTH, N_MOD * D_MODEL), 0.02),
        'g_mix': 1.0 + nrm(ks[10], (DEPTH, D_MODEL), 0.05),
        'g_ffn': 1.0 + nrm(ks[11], (DEPTH, D_MODEL), 0.05),
        'w_in': nrm(ks[12], (DEPTH, D_MODEL, IN_WIDTH), D_MODEL ** -0.5),
        'w_out': nrm(ks[13], (DEPTH, MIX_WIDTH, D_MODEL), MIX_WIDTH ** -0.5),
        'rel_bias': nrm(ks[14], (N_BUCKETS, ATT_HEADS), 0.5),
        'sinks': nrm(ks[15], (DEPTH, ATT_HEADS)),
        'w_pool': nrm(ks[16], (DEPTH, POOL_GROUPS, POOL_GROUP_DIM, POOL_GROUP_DIM), POOL_GROUP_DIM ** -0.5),
        'pool_scale': 1.0 + nrm(ks[17], (DEPTH, POOL_WIDTH), 0.1),
        'w_a2': nrm(ks[18], (DEPTH, GLA_GATE_RANK, GLA_KEY_WIDTH), GLA_GATE_RANK ** -0.5),
        'b_a2': nrm(ks[19], (DEPTH, GLA_KEY_WIDTH), 0.1),
        'g_gla': 1.0 + nrm(ks[20], (DEPTH, GLA_VALUE_WIDTH), 0.05),
        'w_gu': nrm(ks[21], (DEPTH, D_MODEL, 2 * D_FF), D_MODEL ** -0.5),
        'w_down': nrm(ks[22], (DEPTH, D_FF, D_MODEL), D_FF ** -0.5),
        'g_final': 1.0 + nrm(ks[23], (D_MODEL,), 0.05),
    }

def reference(x_prompt, x_sample, cache_win_k, cache_win_v, state_pool, state_gla, c_prompt, c_sample,
              w_ada, b_ada, g_mix, g_ffn, w_in, w_out, rel_bias, sinks, w_pool, pool_scale,
              w_a2, b_a2, g_gla, w_gu, w_down, g_final):
    y_prompt, kp, vp, pp, sp = run_trunk(
        x_prompt, c_prompt, None, None, None, None, 0,
        w_ada, b_ada, g_mix, g_ffn, w_in, w_out, rel_bias, sinks, w_pool, pool_scale,
        w_a2, b_a2, g_gla, w_gu, w_down, g_final)
    y_sample, ks_, vs_, ps_, ss_ = run_trunk(
        x_sample, c_sample, cache_win_k, cache_win_v, state_pool, state_gla, PAST_LEN,
        w_ada, b_ada, g_mix, g_ffn, w_in, w_out, rel_bias, sinks, w_pool, pool_scale,
        w_a2, b_a2, g_gla, w_gu, w_down, g_final)
    return (y_prompt, y_sample, kp, vp, pp, sp, ks_, vs_, ps_, ss_)


_drawn_inputs = setup_inputs


def setup_inputs(seed=0):
    import zlib

    import numpy as np

    out = dict(_drawn_inputs(seed))
    spreads = {}
    factors = {'g_ffn': 4.081, 'rel_bias': 4.451, 'sinks': 23.727, 'pool_scale': 4.315, 'g_gla': 8.0}
    for name, (base, spread) in spreads.items():
        noise = np.random.default_rng([zlib.crc32(name.encode()), seed]).standard_normal(out[name].shape)
        drawn = base * np.exp(spread * noise) if base else spread * noise
        out[name] = __import__('jax').numpy.asarray(drawn.astype(out[name].dtype))
    for name, factor in factors.items():
        out[name] = (out[name] * factor).astype(out[name].dtype)
    return out
```

```python
from contextlib import ExitStack

import numpy as np

import concourse.bass as bass
from concourse import mybir

F32 = mybir.dt.float32
F32R = mybir.dt.float32r
I32 = mybir.dt.int32
ALU = mybir.AluOpType
ACT = mybir.ActivationFunctionType
AX_X = mybir.AxisListType.X

P = 128
D = 2048
KT = D // P
SEQ, DEC_B, DEC_T = 512, 8, 4
HPT, HST = SEQ // 2, DEC_B * DEC_T // 2
HT = HPT + HST
NT = 2 * HT
WIN, HD, KVH, GRP = 128, 64, 2, 4
NB = SEQ // WIN
BUF = 15
GH, DK, DV = 4, 128, 256
RANK = 16
CH = 32
NCH = SEQ // CH
EVAC_AT = 0
GG0_CHUNKS = 13
TAU = 16.0
DFF = 5632
FT = DFF // P
FC = 4
NFC = FT // FC
EPS = 1e-6
NEG = -1e30
NSEQ = 1 + DEC_B * DEC_T
CPITCH = 48
LO_AT = 32

HU = 1024
RAW = 8
HIS = 4
POOL_COLS = 384
LEAD = 3
ADA_V = 8
V_W, M_W = 8 * ADA_V, 8
W_TILES = ("k", "v", "q0", "q1", "block0", "q2", "q3", "block1", "ga")
W_M = {n: M_W + x for x, n in enumerate(W_TILES)}
W_V = {n: V_W + 2 * x + (ADA_V - 2) * sum(b < x for b in (4, 7)) for x, n in enumerate(W_TILES)}
V_U, M_U = W_V["ga"] + 2, W_M["ga"] + 1
V_U_STEP, M_U_STEP = 4 + ADA_V, 3
V_HEAD, M_HEAD = V_U + 2 * V_U_STEP, M_U + 2 * M_U_STEP
V_HEAD_STEP, M_HEAD_STEP = 2 * 6 + 3 * ADA_V, 9
HEAD_M = dict(gq=0, gk=1, block0=2, gv0=3, gv1=4, block1=5, gg0=6, gg1=7, block2=8)
HEAD_V = dict(gq=0, gk=2, block0=4, gv0=12, gv1=14, block1=16, gg0=24, gg1=26, block2=28)
B_W, B_U, B_HEAD = 8, 10, 12
V_OUT, M_OUT = V_HEAD + 4 * V_HEAD_STEP, M_HEAD + 4 * M_HEAD_STEP
V_FFN, M_FFN = V_OUT + 2 * KT, M_OUT + KT
V_CHUNK, M_CHUNK = 2 * 2 * FC + KT * FC // 8, 2 * FC + KT
V_END = V_FFN + V_CHUNK * NFC
V_ALL = V_END + LEAD


def pcol(b, n=WIN):
    per = HPT // n
    return b % per * n + b // per * (HPT + 2 * HST)


def scol(b):
    return HPT + b * DEC_T


H_FIRST = ADA_V * 5 + 4
H_EARLY = (8 * ADA_V - H_FIRST + 4) // ADA_V * 4
SQ_FIRST = 4
SUM_AT = SQ_FIRST + KT + 3
SHARED = range(6 * ADA_V + LEAD, 8 * ADA_V)


def h_tile(v):
    step = v - H_FIRST
    return step // ADA_V * 4 + step % ADA_V if step >= 0 and step % ADA_V < 4 else None


def offsets(parts):
    out, at = {}, 0
    for name, n in parts:
        out[name] = (at, at + n)
        at += n
    return out, at


PRM, PRM_N = offsets([("g_mix", KT), ("g_ffn", KT), ("g_final", KT), ("b_ada", 96),
                      ("sinks", 8), ("sinks_dec", 4), ("c", KT * 9)])
CST, CST_N = offsets([("ident", P), ("ones", P), ("sel", NSEQ), ("chunk_reset", NT), ("chunk_mask", P),
                      ("dec_mask", 32), ("dec_rows", DEC_B), ("dec_cols", DEC_B * 32), ("pool_inv", 64), ("eps", 1)])
HP_AT, HP_N = offsets([("w_pool", P), ("w_a2", P), ("b_a2", 1), ("g_gla", 2), ("pool_scale", 1)])
MSK, MSK_N = offsets([("keep", 256), ("neg", 256), ("keep_dec", 320), ("neg_dec", 320)])


class At:

    def __init__(self, base, i=None, n=0):
        self.base, self.i, self.n = base, i, n

    def __add__(self, k):
        return At(self.base + k, self.i, self.n)

    def val(self, plus=0):
        return self.base + plus if self.i is None else self.i * self.n + (self.base + plus)

    def div(self, m, scale=1, plus=0):
        assert self.i is None or self.n % m == 0
        c = self.base // m * scale + plus
        return c if self.i is None else self.i * (self.n // m * scale) + c

    def mod(self, m):
        assert self.i is None or self.n % m == 0
        return self.base % m


def build(nc, ins, outs):
    with ExitStack() as ctx:
        program(nc, ctx, ins, outs)


def program(nc, ctx, ins, outs):
    base = (nc.sbuf_base + 31) // 32 * 32
    tile_b = NT * 4
    spot = [base]

    def sb(name, shape, dt=F32, at=None):
        n = int(np.prod(shape[1:])) * 4
        if at is None:
            at = spot[0]
            spot[0] = (at + n + 31) // 32 * 32
        return nc.alloc_sbuf_tensor_at(name, shape, dt, offset=at)

    HH = sb("HH", [P, KT, NT], F32R)
    HL = sb("HL", [P, KT, NT], F32R)
    mix_at = spot[0]
    MIX = sb("MIX", [P, KT, NT])
    raw_at = spot[0]
    RW = [sb(f"RW{i}", [P, HU]) for i in range(RAW)]
    WL = [sb(f"WL{i}", [P, HU], F32R, at=raw_at + 4 * HU * i) for i in range(RAW)]
    WH = [sb(f"WH{i}", [P, HU], F32R) for i in range(HIS)]
    MOD = sb("MOD", [P, 6 * KT, NSEQ])
    CS = sb("CS", [P, KT * CPITCH + P], F32R)
    ADAR = sb("ADAR", [64, 512])
    PR = sb("PR", [P, PRM_N])
    CN = sb("CN", [P, CST_N])
    k_at = spot[0]
    KTT = sb("KTT", [P, NT])
    VTT = sb("VTT", [P, NT])
    VTK = sb("VTK", [P, NB + 1, P])
    GA = sb("GA", [P, NT])
    NS = sb("NS", [P, 12])
    SC = sb("SC", [P, 32])
    TB = sb("TB", [P, 1])
    d_at = spot[0]

    QX0 = [sb(f"QX0{i}", [P, NT]) for i in range(4)]
    AC0 = sb("AC0", [P, NT])
    RN0 = sb("RN0", [P, NT])
    TM0 = [sb(f"TM0{i}", [P, NT]) for i in range(4)]
    CSIL = sb("CSIL", [P, KT * 9])
    end0 = spot[0]

    spot[0] = mix_at + 8 * tile_b
    BT = sb("BT", [P, 8, 256])
    KC = sb("KC", [P, DEC_B, WIN])
    VC = sb("VC", [P, DEC_B, P])
    assert spot[0] <= mix_at + KT * tile_b
    spot[0] = d_at
    SBT = sb("SBT", [P, KVH, 2, 160])
    LG = [sb(f"LG{i}", [P, 2, 256]) for i in range(4)]
    PT = [sb(f"PT{i}", [P, 4, P]) for i in range(2)]
    LS = sb("LS", [P, KVH, 2, 160])
    PTN = sb("PTN", [32, 4, P])
    QS = sb("QS", [P, DEC_B, 32])
    UP = sb("UP", [P, 16 + SEQ])
    WA = [sb(f"WA{i}", [P, 16 + SEQ]) for i in range(2)]
    UE = sb("UE", [P, 4, DEC_B, BUF + DEC_T])
    WE = [sb(f"WE{i}", [P, DEC_B, BUF + DEC_T]) for i in range(2)]
    ST = sb("ST", [P, 4, 16])
    STD = sb("STD", [P, 32])
    MK = sb("MK", [P, MSK_N])
    UO = sb("UO", [P, 4, BUF])
    attn_end = spot[0]

    spot[0] = k_at
    GQ = sb("GQ", [P, NT])
    GK = sb("GK", [P, NT])
    KDT = sb("KDT", [P, NB + 1, P])
    spot[0] = d_at
    v_at = spot[0]
    GV = [sb(f"GV{i}", [P, NT]) for i in range(2)]
    GG = [sb(f"GG{i}", [P, NT], at=v_at + i * tile_b) for i in range(2)]
    GVT = sb("GVT", [P, NB + 1, DV])
    gb_at = spot[0]
    GB = sb("GB", [P, NT])
    GT = sb("GT", [P, NT])
    OT = sb("OT", [P, NB, DV], at=gb_at)
    EB = sb("EB", [P, NT])
    en_at = spot[0]
    EN = sb("EN", [P, NT])
    ED = sb("ED", [P, NT])
    KDM = sb("KDM", [32, DEC_B, P], at=en_at)
    QDM = sb("QDM", [P, DEC_B, 32])
    OTD = sb("OTD", [32, DV])
    VR = sb("VR", [P, 3, NB + 1])
    SS = [sb(f"SS{i}", [P, DV]) for i in range(2)]
    SD = sb("SD", [P, DEC_B, DV])
    ATT = sb("ATT", [P, NB, P])
    ATD = sb("ATD", [32, 32])
    HP = sb("HP", [P, HP_N])
    gla_end = spot[0]

    spot[0] = d_at
    X1 = sb("X1", [P, KT, NT])
    x1_end = spot[0]
    assert max(attn_end, gla_end, end0, x1_end) <= nc.sbuf_usable_end, (attn_end, gla_end, end0, nc.sbuf_usable_end)

    spot[0] = mix_at
    AH = sb("AH", [P, FC, NT], F32R)
    AL = sb("AL", [P, FC, NT], F32R)
    tm_at = spot[0]
    SG = [sb(f"SG{i}", [P, NT]) for i in range(2)]
    AF = [sb(f"AF{i}", [P, NT]) for i in range(2)]
    TM1 = [sb(f"TM1{i}", [P, NT], at=tm_at + i * tile_b) for i in range(4)]
    QX = [sb(f"QX{i}", [P, NT]) for i in range(2)]
    AC = sb("AC", [P, NT])
    RN = sb("RN", [P, NT])
    assert spot[0] <= mix_at + KT * tile_b

    PJ = ctx.enter_context(nc.psum_tensor("PJ", [P, 4, 512], F32))
    PS = ctx.enter_context(nc.psum_tensor("PS", [P, 4, 512], F32))

    def prm(name):
        a, b = PRM[name]
        return PR[:, a:b]

    def cst(name):
        a, b = CST[name]
        return CN[:, a:b]

    ident, ones = cst("ident"), cst("ones")
    eps = cst("eps")

    def halves(ap):
        return ap.rearrange("p (a n) -> p a n", a=2)

    def pair(ap, stride, n):
        return bass.AP(ap.tensor, ap.offset, [ap.ap[0], [stride, 2], [1, n]], runtime_checks=ap.runtime_checks,
                       dep_tracking_offset=ap.dep_tracking_offset)

    def prompt(ap):
        return pair(ap, HPT + 2 * HST, HPT)

    def decode(ap):
        return ap[:, HPT:HPT + 2 * HST]

    def bank_prompt(ps):
        return pair(ps, 512 + HST, HPT)

    def o_block(b):
        return PS[:, b // 2, DV * (b % 2):DV * (b % 2) + DV]

    def bank_decode(ps):
        return pair(ps[:, 0, HPT:], 512 - HPT, HST)

    names = (
        "small_in x_in cs_zero csil cs_hi cs_lo neg_sinks "
        "hi lo lo_pool used "
        "ada_rows ada_t mod_scaled "
        "xsq acc sum_done rms rstd nrm nrm_aff nrm_dec h_hi h_lo "
        "masks_in cache_in bias_kept bias_done qs_zero up_zero kv_out v_t v_tok "
        "dec_q_packed dec_scores dec_logits dec_max dec_shift dec_exp dec_sink_exp dec_recip dec_probs dec_turned "
        "dec_by_key dec_values dec_stored "
        "att_scores att_logits att_max att_shift att_exp att_sink_exp att_recip att_probs att_turned att_by_key "
        "att_values att_stored "
        "u_step ue_out pool_mm pool_done "
        "gla_zero head_in state_in gate_mm gate_x gate_abs gate_exp gate_ln log_gate gate_sums to_last exp_b "
        "exp_minus_b exp_to_last "
        "q_decayed q_by_seq k_to_last k_decayed k_turned k_by_token k_by_seq a_mm a_masked gv_turned gv_by_token "
        "chunk_mm state_up out_mm seq_mm seq_up dec_out_mm "
        "out_sq norm_rms norm_r out_scaled_a out_scaled_d out_turned mixed s_out state_out "
        "x1_tmp x1_done x1_acc x1_sq "
        "act_hi act_lo down_a table fin y_out").split()
    S = {n: ctx.enter_context(nc.semaphore(n)) for n in names}
    raw = [ctx.enter_context(nc.semaphore(f"raw{i}")) for i in range(RAW)]
    x1_in = [ctx.enter_context(nc.semaphore(f"x1_in{i}")) for i in range(KT // 4)]
    freed = [ctx.enter_context(nc.semaphore(f"freed{i}")) for i in range(2)]

    def left(m, plus=1):
        return m.div(2, 1, plus)

    U_STEPS = [2 * (q + 1) + 7 for q in range(4)]

    block = ctx.enter_context(nc.Block())

    @block.sync
    def _(sp):
        sp.dma_start(PR[:, :], ins["params"]).then_inc(S["small_in"], 16)
        sp.dma_start(CN[:, :], ins["consts"]).then_inc(S["small_in"], 16)
        for v in range(RAW):
            if v == 4:
                sp.dma_start(MIX[:, :, :], ins["xT"]).then_inc(S["x_in"], 16)
            sp.dma_start(RW[v][:, :], ins["weights"][v]).then_inc(raw[v], 16)

        def load(v):
            sp.wait_ge(S["used"], v.val(1 - RAW))
            sp.dma_start(RW[v.mod(RAW)][:, :], ins["weights"][v.val()]).then_inc(raw[v.mod(RAW)], 16)

        turns = V_ALL // RAW - 1
        with sp.Fori(0, turns) as i:
            for j in range(RAW):
                load(At(RAW + j, i, RAW))
        for v in range(RAW * (turns + 1), V_ALL):
            load(At(v))
        for k in range(KT):
            sp.wait_ge(S["fin"], k + 1)
            sp.dma_start(outs["yT"][:, k, :], X1[:, k, :]).then_inc(S["y_out"], 16)
        sp.wait_ge(S["y_out"], 16 * KT)

    @block.gpsimd
    def _(g):
        g.memset(CS[:, :].bitcast(F32), 0.0).then_inc(S["cs_zero"], 1)

        g.wait_ge(S["xsq"], 2)
        g.tensor_tensor(AC0[:, :], QX0[0][:, :], QX0[1][:, :], ALU.add).then_inc(S["acc"], 1)
        for k in range(2, KT):
            g.wait_ge(S["xsq"], k + 1)
            g.wait_ge(S["acc"], k - 1)
            g.tensor_tensor(AC0[:, :], AC0[:, :], QX0[k % 4][:, :], ALU.add).then_inc(S["acc"], 1)
        g.wait_ge(S["rstd"], 2)
        for k in range(KT):
            g.tensor_tensor(MIX[:, k, :], MIX[:, k, :], RN0[:, :], ALU.mult).then_inc(S["nrm"], 1)

        def lo_share(v):
            g.wait_ge(S["hi"], v.val(1))
            x, n = v.mod(RAW), HU - POOL_COLS
            g.tensor_tensor(WL[x][:, n:], RW[x][:, n:], WH[v.mod(HIS)][:, n:].bitcast(F32), ALU.subtract)\
                .then_inc(S["lo_pool"], 1)

        def h_decode(k):
            td = decode(TM0[k % 4][:, :])
            g.wait_ge(S["nrm"], k + 1)
            g.wait_ge(S["mod_scaled"], k // 4 + 1)
            if k >= 4:
                g.wait_ge(S["h_lo"], k - 3)
            g.tensor_tensor(td, decode(MIX[:, k, :]), MOD[:, KT + k, 1:NSEQ], ALU.mult).then_inc(S["nrm_dec"], 1)
            g.wait_ge(S["nrm_dec"], 2 * k + 1)
            g.tensor_tensor(td, td, MOD[:, k, 1:NSEQ], ALU.add).then_inc(S["nrm_dec"], 1)

        for v in range(H_FIRST, 8 * ADA_V):
            if v + LEAD in SHARED:
                lo_share(At(v + LEAD))
            if h_tile(v) is not None:
                h_decode(h_tile(v))
        for k in range(H_EARLY, KT):
            h_decode(k)

        g.wait_ge(S["h_lo"], KT)
        g.dma_start(BT[:, :, :], ins["bias"]).then_inc(S["masks_in"], 16)
        g.dma_start(SBT[:, :, :, :], ins["bias_dec"]).then_inc(S["masks_in"], 16)
        g.dma_start(MK[:, :], ins["masks"]).then_inc(S["masks_in"], 16)
        g.dma_start(KC[:, :, :], ins["k_cache"]).then_inc(S["cache_in"], 16)
        g.dma_start(VC[:, :, :], ins["v_cache"]).then_inc(S["cache_in"], 16)
        for q in range(4):
            g.dma_start(UE[:, q, :, 0:BUF], ins["pool_state"][:, q]).then_inc(S["cache_in"], 16)
        g.memset(QS[:, :, :], 0.0).then_inc(S["qs_zero"], 1)
        g.memset(UP[:, 0:16], 0.0).then_inc(S["up_zero"], 1)

        g.wait_ge(S["masks_in"], 48)

        def mask(name):
            lo, up = MSK[name]
            return MK[:, lo:up]

        for kv in range(KVH):
            g.tensor_tensor(SBT[:, kv], SBT[:, kv], mask("keep_dec").rearrange("p (g n) -> p g n", g=2), ALU.mult)\
                .then_inc(S["bias_kept"], 1)
        g.tensor_tensor(BT[:, :, :], BT[:, :, :], mask("keep").unsqueeze(1).broadcast_to([P, 8, 256]), ALU.mult)\
            .then_inc(S["bias_kept"], 1)
        g.wait_ge(S["bias_kept"], 3)
        for kv in range(KVH):
            g.tensor_tensor(SBT[:, kv], SBT[:, kv], mask("neg_dec").rearrange("p (g n) -> p g n", g=2), ALU.add)\
                .then_inc(S["bias_done"], 1)
        g.tensor_tensor(BT[:, :, :], BT[:, :, :], mask("neg").unsqueeze(1).broadcast_to([P, 8, 256]), ALU.add)\
            .then_inc(S["bias_done"], 1)

        for m in (At(W_M["k"]), At(W_M["v"])):
            g.wait_ge(freed[m.mod(2)], left(m))
        for n, t in enumerate((KTT, VTT)):
            g.dma_start(outs["kv_prompt"][n], t[:, pcol(NB - 1):pcol(NB - 1) + WIN]).then_inc(S["kv_out"], 16)
            g.dma_start(outs["kv_dec"][n], decode(t[:, :])).then_inc(S["kv_out"], 16)
        g.wait_ge(S["cache_in"], 96)
        g.dma_start(outs["k_past"], KC[:, :, DEC_T:WIN]).then_inc(S["kv_out"], 16)
        g.dma_start(outs["v_past"], VC[DEC_T:WIN, :, :]).then_inc(S["kv_out"], 16)

        step = 0
        for q in range(4):
            m = At(M_U + q // 2 * M_U_STEP + q % 2)
            g.wait_ge(freed[m.mod(2)], left(m))
            cur, cur_e = UP, UE[:, q]
            for i in range(q + 1):
                n, lo = 1 << i, 2 << i
                if step:
                    g.wait_ge(S["u_step"], step)
                g.tensor_tensor(WA[i % 2][:, lo:], cur[:, lo:], cur[:, lo - n:16 + SEQ - n], ALU.add)\
                    .then_inc(S["u_step"], 1)
                g.tensor_tensor(WE[i % 2][:, :, lo - 1:], cur_e[:, :, lo - 1:],
                                cur_e[:, :, lo - 1 - n:BUF + DEC_T - n], ALU.add).then_inc(S["u_step"], 1)
                step += 2
                cur, cur_e = WA[i % 2], WE[i % 2]
            g.wait_ge(S["u_step"], step)
            lo, up = CST["pool_inv"]
            g.tensor_tensor(cur[:, 16:32], cur[:, 16:32], CN[:, lo + 16 * q:lo + 16 * q + 16], ALU.mult)\
                .then_inc(S["u_step"], 1)
            g.tensor_scalar(cur[:, 32:], cur[:, 32:], 1.0 / (2 << q), None, ALU.mult).then_inc(S["u_step"], 1)
            g.tensor_scalar(cur_e[:, :, BUF:], cur_e[:, :, BUF:], 1.0 / (2 << q), None, ALU.mult)\
                .then_inc(S["u_step"], 1)
            step += 3
            g.wait_ge(S["u_step"], step)
            g.tensor_tensor(prompt(MIX[:, 4 + q, :]), cur[:, 16:].rearrange("p (a n) -> p a n", a=2),
                            UP[:, 16:].rearrange("p (a n) -> p a n", a=2), ALU.subtract).then_inc(S["u_step"], 1)
            for a in range(2):
                g.tensor_tensor(MIX[:, 4 + q, scol(4 * a):scol(4 * a) + HST].rearrange("p (b t) -> p b t", t=DEC_T),
                                cur_e[:, 4 * a:4 * a + 4, BUF:], UE[:, q, 4 * a:4 * a + 4, BUF:], ALU.subtract)\
                    .then_inc(S["u_step"], 1)
            g.tensor_copy(UO[:, q, :], UP[:, 16 + SEQ - BUF:]).then_inc(S["u_step"], 1)
            step += 4
        assert step == sum(U_STEPS)
        g.wait_ge(S["u_step"], step)
        for q in range(4):
            g.dma_start(outs["pool_dec"][:, q], UE[:, q, :, DEC_T:]).then_inc(S["ue_out"], 16)
        g.dma_start(outs["pool_prompt"], UO[:, :, :]).then_inc(S["ue_out"], 16)

        g.wait_ge(S["att_stored"], NB)
        g.wait_ge(S["kv_out"], 16 * 6)
        g.wait_ge(S["ue_out"], 80)
        g.memset(ATT[:, :, :], 0.0).then_inc(S["gla_zero"], 1)
        g.memset(ATD[:, :], 0.0).then_inc(S["gla_zero"], 1)
        g.memset(VR[:, :, :], 0.0).then_inc(S["gla_zero"], 1)
        with g.Fori(0, GH // 2) as i:
            for r in range(2):
                h = At(r, i, 2)
                g.dma_start(HP[:, :], ins["head_params"][h.val()]).then_inc(S["head_in"], 16)
                g.dma_start(SD[:, :, :], ins["gla_state"][h.val()]).then_inc(S["state_in"], 16)
                for n in range(3):
                    v = At(V_HEAD + V_HEAD_STEP * r + HEAD_V[f"block{n}"], i, 2 * V_HEAD_STEP)
                    if n == 2:
                        g.wait_ge(S["state_up"], At(NCH * r, i, 2 * NCH).val(NCH))
                        g.wait_ge(S["seq_up"], At(DEC_B * r, i, 2 * DEC_B).val(DEC_B))
                        g.dma_start(outs["gla_prompt"][h.val()], SS[0][:, :]).then_inc(S["s_out"], 16)
                        g.dma_start(outs["gla_dec"][h.val()], SD[:, :, :]).then_inc(S["state_out"], 16)
                    for s in range(ADA_V - LEAD):
                        lo_share(v + (s + LEAD))
                g.wait_ge(S["s_out"], At(16 * r, i, 32).val(16))
                g.wait_ge(S["state_out"], At(16 * r, i, 32).val(16))
                g.wait_ge(S["mixed"], At(2 * r, i, 4).val(2))

        for k in range(0, KT, 4):
            g.dma_start(X1[:, k:k + 4, :], ins["xT"][:, k:k + 4, :]).then_inc(x1_in[k // 4], 16)

        def sum_tiles(r):
            g.memset(AC[:, :], 0.0).then_inc(S["x1_acc"], 1)

            def add(k):
                g.wait_ge(S["x1_sq"], k.val(1))
                g.wait_ge(S["x1_acc"], k.val(1))
                g.tensor_tensor(AC[:, :], AC[:, :], QX[k.mod(2)][:, :], ALU.add).then_inc(S["x1_acc"], 1)

            with g.Fori(0, KT // 2 - 1) as i:
                for j in range(2):
                    add(At(r * KT + j, i, 2))
            add(At(r * KT + KT - 2))

        g.wait_ge(S["h_lo"], 2 * KT)
        sum_tiles(0)
        g.wait_ge(S["mod_scaled"], 5)
        for k in range(KT):
            td = decode(TM1[k % 4][:, :])
            g.wait_ge(S["nrm"], KT + k + 1)
            g.tensor_tensor(td, td, MOD[:, 4 * KT + k, 1:NSEQ], ALU.mult).then_inc(S["nrm_dec"], 1)
            g.wait_ge(S["nrm_dec"], 2 * (KT + k) + 1)
            g.tensor_tensor(td, td, MOD[:, 3 * KT + k, 1:NSEQ], ALU.add).then_inc(S["nrm_dec"], 1)
        g.wait_ge(S["sum_done"], 3)
        sum_tiles(1)

    @block.scalar
    def _(a):
        def hi(v):
            a.wait_ge(raw[v.mod(RAW)], v.div(RAW, 16, 16))
            if v.i is not None or v.base >= HIS:
                a.wait_ge(S["used"], v.val(1 - HIS))
            a.activation(WH[v.mod(HIS)][:, :], RW[v.mod(RAW)][:, :], ACT.Copy).then_inc(S["hi"], 1)

        def banks(m):
            return PJ[:, 2 * m.mod(2):2 * m.mod(2) + 2, 0:HT]

        def evacuate(m, v, dst, func=ACT.Copy):
            a.wait_ge(S["used"], v.val(1))
            a.activation(halves(dst), banks(m), func).then_inc(freed[m.mod(2)], 1)

        def rows(m, v, b):
            a.wait_ge(S["used"], v.val(1))
            if b.i is not None or b.base:
                a.wait_ge(S["ada_t"], b.val())
            a.activation(ADAR[:, :], PJ[0:64, 2 * m.mod(2), :], ACT.Copy).then_inc(S["ada_rows"], 1)

        def ada_block(m, v, b, jobs=None):
            for s in range(ADA_V):
                hi(v + (s + LEAD))
                if s in (jobs or {}):
                    jobs[s]()
            rows(m, v + (ADA_V - 1), b)

        def h_hi(k):
            a.wait_ge(S["nrm_aff"], k + 1)
            a.wait_ge(S["nrm_dec"], 2 * (k + 1))
            a.activation(HH[:, k, :], TM0[k % 4][:, :], ACT.Copy).then_inc(S["h_hi"], 1)

        a.wait_ge(S["small_in"], 32)
        a.activation(CSIL[:, :], prm("c"), ACT.Silu).then_inc(S["csil"], 1)
        a.wait_ge(S["csil"], 1)
        a.wait_ge(S["cs_zero"], 1)
        a.activation(CS[:, 0:KT * CPITCH].rearrange("p (k c) -> p k c", c=CPITCH)[:, :, 0:9],
                     CSIL[:, :].rearrange("p (k c) -> p k c", c=9), ACT.Copy).then_inc(S["cs_hi"], 1)
        for v in range(LEAD):
            hi(At(v))
        for b in range(8):
            for s in range(ADA_V):
                hi(At(ADA_V * b + s + LEAD))
                if b and s == 1:
                    rows(At(b - 1), At(ADA_V * b - 1), At(b - 1))
                k = ADA_V * b + s - SQ_FIRST
                if 0 <= k < KT:
                    if k == 0:
                        a.wait_ge(S["x_in"], 16)
                    if k >= 4:
                        a.wait_ge(S["acc"], k - 4 if k > 4 else 1)
                    a.activation(QX0[k % 4][:, :], MIX[:, k, :], ACT.Square).then_inc(S["xsq"], 1)
                if ADA_V * b + s == SUM_AT + 1:
                    a.wait_ge(S["sum_done"], 1)
                    a.activation(halves(RN0[:, :]), PS[:, 0:2, 0:HT], ACT.Sqrt, bias=eps, scale=1.0 / D)\
                        .then_inc(S["rms"], 1)
                if h_tile(ADA_V * b + s - 1) is not None:
                    h_hi(h_tile(ADA_V * b + s - 1))
        h_hi(H_EARLY - 1)
        rows(At(7), At(ADA_V * 8 - 1), At(7))
        for k in range(H_EARLY, KT):
            h_hi(k)

        for n in range(4):
            hi(At(V_W + n + LEAD))
        evacuate(At(W_M["k"]), At(V_W + 3), KTT[:, :])
        evacuate(At(W_M["v"]), At(V_W + 3), VTT[:, :])
        for name in W_TILES[2:]:
            m, v = At(W_M[name]), At(W_V[name])
            if name[0] == "b":
                ada_block(m, v, At(B_W + int(name[5])))
                continue
            hi(v + LEAD)
            if name == "q0":
                a.wait_ge(S["v_t"], 1)
                a.activation(VTK[:, 0:NB, :], PS[:, 0, :].rearrange("p (b d) -> p b d", b=NB), ACT.Copy)\
                    .then_inc(S["v_tok"], 1)
                a.wait_ge(S["v_t"], 2)
                a.activation(VTK[0:32, NB, :], PS[0:32, 1, 0:P], ACT.Copy).then_inc(S["v_tok"], 1)
            if name == "ga":
                a.wait_ge(S["dec_shift"], 1)
                for i in range(4):
                    a.activation(LS[:, i // 2, i % 2], LS[:, i // 2, i % 2], ACT.Exp, bias=STD[:, i:i + 1],
                                 accum_out=STD[:, 8 + i:9 + i]).then_inc(S["dec_exp"], 1)
                a.activation(STD[:, 16:20], STD[:, 12:16], ACT.Exp).then_inc(S["dec_sink_exp"], 1)
            hi(v + (1 + LEAD))
            if name == "ga":
                a.wait_ge(S["dec_turned"], 1)
                a.activation(PT[0][:, :, :], PS[:, 2, :].rearrange("p (n c) -> p n c", n=4), ACT.Copy)\
                    .then_inc(S["dec_by_key"], 1)
                a.wait_ge(S["dec_turned"], 2)
                a.activation(PTN[:, :, :], PS[0:32, 3, :].rearrange("p (n c) -> p n c", n=4), ACT.Copy)\
                    .then_inc(S["dec_by_key"], 1)
            evacuate(m, v + 1, GA[:, :] if name == "ga" else MIX[:, int(name[1]), :])
        m, v = At(M_U), At(V_U)

        def turned(job, k0):
            a.wait_ge(S["att_turned"], job + 1)
            if job >= 2:
                a.wait_ge(S["att_values"], job - 1)
            else:
                a.wait_ge(S["dec_stored"], 1)
            a.activation(PT[job % 2][:, :, :].rearrange("p (j k) c -> p j k c", j=2)[:, :, k0:],
                         PS[:, 2, :].rearrange("p (j k c) -> p j k c", j=2, k=2)[:, :, k0:], ACT.Copy)\
                .then_inc(S["att_by_key"], 1)

        for q in range(4):
            k0 = 1 if q == 0 else 0
            for n in range(4):
                job = 4 * q + n
                st = ST[:, n]
                a.wait_ge(S["att_shift"], job + 1)
                for j in range(2):
                    a.activation(LG[n][:, j, 128 * k0:], LG[n][:, j, 128 * k0:], ACT.Exp, bias=st[:, j:j + 1],
                                 accum_out=st[:, 4 + j:5 + j]).then_inc(S["att_exp"], 1)
                a.activation(st[:, 6:8], st[:, 2:4], ACT.Exp).then_inc(S["att_sink_exp"], 1)
                if n == 0:
                    hi(v + LEAD)
                else:
                    turned(job - 1, k0)
            turned(4 * q + 3, k0)
            hi(v + (1 + LEAD))
            if q:
                a.wait_ge(S["u_step"], sum(U_STEPS[:q]))
            else:
                a.wait_ge(S["up_zero"], 1)
                a.wait_ge(S["cache_in"], 96)
            a.wait_ge(S["used"], v.val(2))
            a.activation(UP[:, 16:].rearrange("p (a n) -> p a n", a=2), bank_prompt(banks(m)), ACT.Copy)
            a.activation(UE[:, q, 0:4, BUF:], PJ[:, 2 * m.mod(2), HPT:HT].rearrange("p (b t) -> p b t", t=DEC_T),
                         ACT.Copy)
            a.activation(UE[:, q, 4:8, BUF:], PJ[:, 2 * m.mod(2) + 1, 0:HST].rearrange("p (b t) -> p b t", t=DEC_T),
                         ACT.Copy).then_inc(freed[m.mod(2)], 1)
            m, v = m + 1, v + 2
            if q % 2:
                ada_block(m, v, At(B_U + q // 2))
                m, v = m + 1, v + ADA_V

        with a.Fori(0, GH // 2) as i:
            for r in range(2):
                h, two, four = At(r, i, 2), At(2 * r, i, 4), At(4 * r, i, 8)

                def at(name):
                    return (At(M_HEAD + M_HEAD_STEP * r + HEAD_M[name], i, 2 * M_HEAD_STEP),
                            At(V_HEAD + V_HEAD_STEP * r + HEAD_V[name], i, 2 * V_HEAD_STEP))

                def block_of(n):
                    return At(B_HEAD + 3 * r + n, i, 6)

                def by_token(e):
                    a.wait_ge(S["gv_turned"], four.val(2 * e + 1))
                    a.activation(GVT[:, 0:NB, P * e:P * e + P], PS[:, 0, :].rearrange("p (b d) -> p b d", b=NB),
                                 ACT.Copy).then_inc(S["gv_by_token"], 1)
                    a.wait_ge(S["gv_turned"], four.val(2 * e + 2))
                    a.activation(GVT[0:32, NB, P * e:P * e + P], PS[0:32, 1, 0:P], ACT.Copy).then_inc(S["gv_by_token"], 1)

                m, v = at("gq")
                hi(v + LEAD)
                hi(v + (1 + LEAD))
                a.wait_ge(S["gla_zero"], 3)
                evacuate(m, v + 1, GQ[:, :])
                m, v = at("gk")
                hi(v + LEAD)
                a.wait_ge(S["pool_mm"], h.val(1))
                a.wait_ge(S["u_step"], sum(U_STEPS))
                a.activation(halves(MIX[:, h.val(4), :]), PS[:, 2:4, 0:HT], ACT.Identity,
                             scale=HP[:, HP_AT["pool_scale"][0]:HP_AT["pool_scale"][1]]).then_inc(S["pool_done"], 1)
                a.wait_ge(S["gate_abs"], h.val(1))
                a.activation(GT[:, :], GT[:, :], ACT.Exp, scale=-1.0).then_inc(S["gate_exp"], 1)
                a.wait_ge(S["gate_exp"], h.val(1))
                a.activation(GT[:, :], GT[:, :], ACT.Ln, bias=ones[:, 0:1]).then_inc(S["gate_ln"], 1)
                hi(v + (1 + LEAD))
                a.wait_ge(S["gate_sums"], h.val(1))
                a.activation(EB[:, :], GT[:, :], ACT.Exp, scale=1.0 / TAU).then_inc(S["exp_b"], 1)
                a.activation(EN[:, :], GT[:, :], ACT.Exp, scale=-1.0 / TAU).then_inc(S["exp_minus_b"], 1)
                a.wait_ge(S["to_last"], two.val(2))
                a.activation(ED[:, :], ED[:, :], ACT.Exp, scale=1.0 / TAU).then_inc(S["exp_to_last"], 1)
                ada_block(*at("block0"), block_of(0), {EVAC_AT: lambda m=m, v=v: evacuate(m, v + 1, GK[:, :])})
                m, v = at("gv0")
                hi(v + LEAD)
                a.wait_ge(S["k_turned"], two.val(1))
                a.activation(KDT[:, 0:NB, :], PS[:, 0, :].rearrange("p (b d) -> p b d", b=NB), ACT.Copy)\
                    .then_inc(S["k_by_token"], 1)
                a.wait_ge(S["k_turned"], two.val(2))
                a.activation(KDT[0:32, NB, :], PS[0:32, 1, 0:P], ACT.Copy).then_inc(S["k_by_token"], 1)
                hi(v + (1 + LEAD))
                evacuate(m, v + 1, GV[0][:, :])
                m, v = at("gv1")
                hi(v + LEAD)
                by_token(0)
                hi(v + (1 + LEAD))
                ada_block(*at("block1"), block_of(1), {EVAC_AT: lambda m=m, v=v: evacuate(m, v + 1, GV[1][:, :]),
                                                       3: lambda: by_token(1)})
                m, v = at("gg0")
                hi(v + LEAD)
                hi(v + (1 + LEAD))
                evacuate(m, v + 1, GG[0][:, :], ACT.Silu)
                m, v = at("gg1")
                hi(v + LEAD)
                a.wait_ge(S["out_mm"], h.val(1))
                for b in range(NB):
                    a.activation(OT[:, b, :], o_block(b), ACT.Square, accum_out=VR[:, 0, b:b + 1])\
                        .then_inc(S["out_sq"], 1)
                hi(v + (1 + LEAD))
                a.wait_ge(S["dec_out_mm"], h.val(1))
                a.activation(OTD[:, :], PS[0:32, 3, 0:DV], ACT.Square, accum_out=VR[0:32, 0, NB:NB + 1])\
                    .then_inc(S["out_sq"], 1)
                a.wait_ge(S["out_sq"], At((NB + 1) * r, i, 2 * (NB + 1)).val(NB + 1))
                a.activation(VR[:, 1, :], VR[:, 0, :], ACT.Sqrt, bias=eps, scale=1.0 / DV).then_inc(S["norm_rms"], 1)
                a.wait_ge(S["norm_r"], h.val(1))
                for b in range(NB // 2):
                    a.activation(OT[:, b, :], o_block(b), ACT.Copy, scale=VR[:, 2, b:b + 1]).then_inc(S["out_scaled_a"], 1)
                a.activation(OTD[:, :], PS[0:32, 3, 0:DV], ACT.Copy, scale=VR[0:32, 2, NB:NB + 1])\
                    .then_inc(S["out_scaled_a"], 1)
                ada_block(*at("block2"), block_of(2),
                          {EVAC_AT: lambda m=m, v=v: evacuate(m, v + 1, GG[1][:, :], ACT.Silu)})

        for k in range(KT):
            a.wait_ge(S["mixed"], 2 * GH - (KT - 1 - k if k >= KT - 2 else 2))
            a.activation(HH[:, k, :], MIX[:, k, :], ACT.Copy).then_inc(S["h_hi"], 1)

        def square_x1(k, r):
            a.wait_ge(S["x1_done"], (KT * NFC if r else 0) + k + 1)
            a.wait_ge(S["x1_acc"], r * KT + max(k, 1))
            if k == 1 and r:
                a.wait_ge(S["sum_done"], 3)
            a.activation(QX[k % 2][:, :], X1[:, k, :], ACT.Square).then_inc(S["x1_sq"], 1)

        for k in range(KT):
            v = At(V_OUT + 2 * k)
            hi(v + LEAD)
            hi(v + (1 + LEAD))
            if k:
                square_x1(k - 1, 0)
        a.activation(TB[:, :], eps, ACT.Sqrt).then_inc(S["table"], 1)
        square_x1(KT - 1, 0)
        a.wait_ge(S["mod_scaled"], 5)
        for w in range(2):
            a.wait_ge(S["sum_done"], 2 + w)
            a.activation(RN[:, HT * w:HT * w + HT], PS[:, w, 0:HT], ACT.Sqrt, bias=eps, scale=1.0 / D)\
                .then_inc(S["rms"], 1)
        for k in range(KT):
            t = TM1[k % 4]
            a.wait_ge(S["nrm"], KT + k + 1)
            a.activation(prompt(t[:, :]), prompt(t[:, :]), ACT.Identity, bias=MOD[:, 3 * KT + k, 0:1],
                         scale=MOD[:, 4 * KT + k, 0:1]).then_inc(S["nrm_aff"], 1)
            a.wait_ge(S["nrm_aff"], KT + k + 1)
            a.wait_ge(S["nrm_dec"], 2 * (KT + k + 1))
            a.activation(HH[:, k, :], t[:, :], ACT.Copy).then_inc(S["h_hi"], 1)

        def chunk(i, last):
            for f in range(FC):
                m, v = At(M_FFN + 2 * f, i, M_CHUNK), At(V_FFN + 4 * f, i, V_CHUNK)
                hi(v + LEAD)
                hi(v + (1 + LEAD))
                evacuate(m, v + 2, SG[f % 2][:, :], ACT.Silu)
                hi(v + (2 + LEAD))
                hi(v + (3 + LEAD))
                m = m + 1
                a.wait_ge(freed[m.mod(2)], left(m))
                a.activation(AH[:, f, :], AF[f % 2][:, :], ACT.Copy).then_inc(S["act_hi"], 1)
            for u in range(KT // 2):
                hi(At(V_FFN + 4 * FC + u + LEAD, i, V_CHUNK))
                if last and u:
                    square_x1(2 * u - 2, 1)
                    square_x1(2 * u - 1, 1)

        with a.Fori(0, NFC - 1) as i:
            chunk(i, False)
        chunk(NFC - 1, True)
        square_x1(KT - 2, 1)
        a.wait_ge(S["table"], 1)
        a.activation(TB[:, :], eps, ACT.Sqrt).then_inc(S["table"], 1)
        square_x1(KT - 1, 1)
        for w in range(2):
            a.wait_ge(S["sum_done"], 4 + w)
            a.activation(RN[:, HT * w:HT * w + HT], PS[:, w, 0:HT], ACT.Sqrt, bias=eps, scale=1.0 / D)\
                .then_inc(S["rms"], 1)

    @block.vector
    def _(d):
        def lo(v, n=HU):
            d.wait_ge(S["hi"], v.val(1))
            d.tensor_tensor(WL[v.mod(RAW)][:, 0:n], RW[v.mod(RAW)][:, 0:n], WH[v.mod(HIS)][:, 0:n].bitcast(F32),
                            ALU.subtract).then_inc(S["lo"], 1)

        def banks(m):
            return PJ[:, 2 * m.mod(2):2 * m.mod(2) + 2, 0:HT]

        def mod_block(m, b):
            d.wait_ge(S["ada_t"], b.val(1))
            four = At(4 * b.base, b.i, 4 * b.n)
            at = PRM["b_ada"][0]
            d.tensor_tensor(MOD[:, bass.ds(four.val(), 4), :],
                            PJ[:, 2 * m.mod(2) + 1, 0:4 * NSEQ].rearrange("p (f s) -> p f s", f=4),
                            PR[:, bass.ds(four.val(at), 4)].unsqueeze(2).broadcast_to([P, 4, NSEQ]), ALU.add)\
                .then_inc(freed[m.mod(2)], 1)

        def scale_by(m, gain, first, n, k):
            d.wait_ge(freed[m.mod(2)], left(m))
            mod = MOD[:, first:first + n, :]
            d.scalar_tensor_tensor(out=mod, in0=mod, scalar=1.0,
                                   in1=prm(gain)[:, k:k + n].unsqueeze(2).broadcast_to([P, n, NSEQ]),
                                   op0=ALU.add, op1=ALU.mult).then_inc(S["mod_scaled"], 1)

        def h_aff(k):
            d.wait_ge(S["nrm"], k + 1)
            d.wait_ge(S["mod_scaled"], k // 4 + 1)
            if k >= 4:
                d.wait_ge(S["h_lo"], k - 3)
            d.tensor_scalar(prompt(TM0[k % 4][:, :]), prompt(MIX[:, k, :]), MOD[:, KT + k, 0:1], MOD[:, k, 0:1],
                            ALU.mult, ALU.add).then_inc(S["nrm_aff"], 1)

        def h_lo(k):
            d.wait_ge(S["h_hi"], k + 1)
            d.tensor_tensor(HL[:, k, :], TM0[k % 4][:, :], HH[:, k, :].bitcast(F32), ALU.subtract)\
                .then_inc(S["h_lo"], 1)

        d.wait_ge(S["small_in"], 32)
        d.tensor_scalar(NS[:, :], PR[:, PRM["sinks"][0]:PRM["sinks_dec"][1]], -1.0, None, ALU.mult)\
            .then_inc(S["neg_sinks"], 1)
        cs = CS[:, 0:KT * CPITCH].rearrange("p (k c) -> p k c", c=CPITCH)
        d.wait_ge(S["cs_hi"], 1)
        d.tensor_tensor(cs[:, :, LO_AT:LO_AT + 9], CSIL[:, :].rearrange("p (k c) -> p k c", c=9),
                        cs[:, :, 0:9].bitcast(F32), ALU.subtract).then_inc(S["cs_lo"], 1)
        for v in range(LEAD):
            lo(At(v))

        def block_done(b):
            mod_block(At(b), At(b))
            if b >= 4:
                scale_by(At(b), "g_mix", KT + 4 * (b - 4), 4, 4 * (b - 4))

        for b in range(8):
            for s in range(ADA_V):
                v = ADA_V * b + s + LEAD
                lo(At(v), HU - POOL_COLS if v in SHARED else HU)
                if b and s == 3:
                    block_done(b - 1)
                if ADA_V * b + s == SUM_AT + 2:
                    d.wait_ge(S["rms"], 1)
                    d.reciprocal(RN0[:, 0:HT], RN0[:, 0:HT]).then_inc(S["rstd"], 1)
                if ADA_V * b + s == SUM_AT + 4:
                    d.reciprocal(RN0[:, HT:NT], RN0[:, HT:NT]).then_inc(S["rstd"], 1)
                if h_tile(ADA_V * b + s) is not None:
                    h_aff(h_tile(ADA_V * b + s))
                if h_tile(ADA_V * b + s - 2) is not None:
                    h_lo(h_tile(ADA_V * b + s - 2))
        for k in range(H_EARLY - 2, H_EARLY):
            h_lo(k)
        block_done(7)
        h_aff(H_EARLY)
        h_aff(H_EARLY + 1)
        for k in range(H_EARLY, KT):
            if k + 2 < KT:
                h_aff(k + 2)
            h_lo(k)

        for n in range(4):
            lo(At(V_W + n + LEAD))
        for name in W_TILES[2:]:
            m, v = At(W_M[name]), At(W_V[name])
            if name[0] == "b":
                for s in range(ADA_V):
                    lo(v + (s + LEAD))
                continue
            lo(v + LEAD)
            if name in ("q2", "ga"):
                mod_block(m + -1, At(B_W + (name == "ga")))
            if name == "ga":
                d.wait_ge(freed[W_M["q3"] % 2], left(At(W_M["q3"])))
                d.wait_ge(S["qs_zero"], 1)
                for w in range(2):
                    d.tensor_copy(QS[:, 4 * w:4 * w + 4, 0:16].rearrange("p b (t j) -> p j b t", j=GRP),
                                  MIX[:, 0:4, scol(4 * w):scol(4 * w) + HST].rearrange("p j (b t) -> p j b t", t=DEC_T))\
                        .then_inc(S["dec_q_packed"], 1)
                d.wait_ge(S["bias_done"], 3)
                for kv in range(KVH):
                    d.wait_ge(S["dec_scores"], kv + 1)
                    d.scalar_tensor_tensor(out=LS[:, kv].rearrange("p g n -> p (g n)"), in0=PS[:, kv, 0:320],
                                           scalar=HD ** -0.5, in1=SBT[:, kv].rearrange("p g n -> p (g n)"),
                                           op0=ALU.mult, op1=ALU.add).then_inc(S["dec_logits"], 1)
                d.wait_ge(S["dec_logits"], 2)
                ls = LS[:, :, :, :].rearrange("p k g n -> p (k g) n")
                d.tensor_reduce(STD[:, 4:8], ls, AX_X, ALU.max).then_inc(S["dec_max"], 1)
                d.wait_ge(S["dec_max"], 1)
                d.wait_ge(S["neg_sinks"], 1)
                d.scalar_tensor_tensor(out=STD[:, 0:4], in0=STD[:, 4:8], scalar=-1.0, in1=NS[:, 8:12],
                                       op0=ALU.mult, op1=ALU.min).then_inc(S["dec_max"], 1)
                d.wait_ge(S["dec_max"], 2)
                d.tensor_tensor(STD[:, 12:16], STD[:, 0:4], NS[:, 8:12], ALU.subtract).then_inc(S["dec_shift"], 1)
                d.wait_ge(S["dec_exp"], 4)
                d.wait_ge(S["dec_sink_exp"], 1)
                d.tensor_tensor(STD[:, 20:24], STD[:, 8:12], STD[:, 16:20], ALU.add).then_inc(S["dec_recip"], 1)
                d.wait_ge(S["dec_recip"], 1)
                d.reciprocal(STD[:, 24:28], STD[:, 20:24]).then_inc(S["dec_recip"], 1)
                d.wait_ge(S["dec_recip"], 2)
                d.tensor_tensor(ls, ls, STD[:, 24:28].unsqueeze(2).broadcast_to([P, 4, 160]), ALU.mult)\
                    .then_inc(S["dec_probs"], 1)
                lo(v + (1 + LEAD))
                d.wait_ge(S["dec_values"], 1)
                for w in range(2):
                    d.tensor_copy(MIX[:, 0:4, scol(4 * w):scol(4 * w) + HST].rearrange("p j (b t) -> p j b t", t=DEC_T),
                                  PS[:, 0, 64 * w:64 * w + 64].rearrange("p (b t j) -> p j b t", b=4, j=GRP))\
                        .then_inc(S["dec_stored"], 1)
            else:
                lo(v + (1 + LEAD))

        def normalise(job, k0):
            st, lg = ST[:, job % 4], LG[job % 4]
            d.wait_ge(S["att_exp"], 2 * job + 2)
            d.wait_ge(S["att_sink_exp"], job + 1)
            d.tensor_tensor(st[:, 10:12], st[:, 4:6], st[:, 6:8], ALU.add).then_inc(S["att_recip"], 1)
            d.wait_ge(S["att_recip"], 2 * job + 1)
            d.reciprocal(st[:, 12:14], st[:, 10:12]).then_inc(S["att_recip"], 1)
            d.wait_ge(S["att_recip"], 2 * job + 2)
            for j in range(2):
                d.tensor_scalar(lg[:, j, 128 * k0:], lg[:, j, 128 * k0:], st[:, 12 + j:13 + j], None, ALU.mult)\
                    .then_inc(S["att_probs"], 1)

        m, v = At(M_U), At(V_U)
        for q in range(4):
            k0 = 1 if q == 0 else 0
            if q == 2:
                mod_block(m + -1, At(B_U))
            for n in range(4):
                job, kv, pair = 4 * q + n, n % 2, n // 2
                st, lg = ST[:, n], LG[n][:, :, 128 * k0:]
                head = GRP * kv + 2 * pair
                d.wait_ge(S["att_scores"], job + 1)
                if job >= 4:
                    d.wait_ge(S["att_turned"], job - 3)
                d.scalar_tensor_tensor(out=lg, in0=PS[:, n % 2, :].rearrange("p (j k) -> p j k", j=2)[:, :, 128 * k0:],
                                       scalar=HD ** -0.5, in1=BT[:, head:head + 2, 128 * k0:],
                                       op0=ALU.mult, op1=ALU.add).then_inc(S["att_logits"], 1)
                d.wait_ge(S["att_logits"], job + 1)
                d.tensor_reduce(st[:, 8:10], lg, AX_X, ALU.max).then_inc(S["att_max"], 1)
                d.wait_ge(S["att_max"], 2 * job + 1)
                d.scalar_tensor_tensor(out=st[:, 0:2], in0=st[:, 8:10], scalar=-1.0, in1=NS[:, head:head + 2],
                                       op0=ALU.mult, op1=ALU.min).then_inc(S["att_max"], 1)
                d.wait_ge(S["att_max"], 2 * job + 2)
                d.tensor_tensor(st[:, 2:4], st[:, 0:2], NS[:, head:head + 2], ALU.subtract).then_inc(S["att_shift"], 1)
                if n:
                    normalise(job - 1, k0)
                if n == 1:
                    lo(v + LEAD)
            normalise(4 * q + 3, k0)
            lo(v + (1 + LEAD))
            d.wait_ge(S["att_values"], 4 * q + 4)
            d.tensor_copy(MIX[:, 0:4, pcol(q):pcol(q) + WIN], PS[:, 3, :].rearrange("p (j c) -> p j c", j=4))\
                .then_inc(S["att_stored"], 1)
            m, v = m + 1, v + 2
            if q % 2:
                for s in range(ADA_V):
                    lo(v + (s + LEAD))
                m, v = m + 1, v + ADA_V

        with d.Fori(0, GH // 2) as i:
            for r in range(2):
                h, two = At(r, i, 2), At(2 * r, i, 4)
                chunks = At(NCH * r, i, 2 * NCH)

                def at(name):
                    return (At(M_HEAD + M_HEAD_STEP * r + HEAD_M[name], i, 2 * M_HEAD_STEP),
                            At(V_HEAD + V_HEAD_STEP * r + HEAD_V[name], i, 2 * V_HEAD_STEP))

                def block_of(n):
                    return At(B_HEAD + 3 * r + n, i, 6)

                def update(c):
                    last = pcol(c, CH) + CH - 1
                    d.wait_ge(S["chunk_mm"], chunks.val(c + 1))
                    if c == 0:
                        d.tensor_copy(SS[1][:, :], PS[:, 2, 0:DV]).then_inc(S["state_up"], 1)
                        return
                    if c == 1:
                        d.wait_ge(S["head_in"], At(16 * r, i, 32).val(16))
                    d.wait_ge(S["state_up"], chunks.val(c))
                    d.scalar_tensor_tensor(out=SS[(c + 1) % 2][:, :], in0=SS[c % 2][:, :], scalar=EB[:, last:last + 1],
                                           in1=PS[:, 2 + c % 2, 0:DV], op0=ALU.mult, op1=ALU.add)\
                        .then_inc(S["state_up"], 1)

                m, v = at("gq")
                lo(v + LEAD)
                mod_block(m + -1, block_of(-1))
                lo(v + (1 + LEAD))
                v = at("gk")[1]
                lo(v + LEAD)
                d.wait_ge(S["gla_zero"], 3)
                d.wait_ge(S["gate_mm"], h.val(1))
                d.tensor_scalar(halves(GB[:, :]), PS[:, 0:2, 0:HT], HP[:, HP_AT["b_a2"][0]:HP_AT["b_a2"][1]], None,
                                ALU.add).then_inc(S["gate_x"], 1)
                d.wait_ge(S["gate_x"], h.val(1))
                d.scalar_tensor_tensor(out=GT[:, :], in0=GB[:, :], scalar=-1.0, in1=GB[:, :], op0=ALU.mult,
                                       op1=ALU.max).then_inc(S["gate_abs"], 1)
                d.wait_ge(S["gate_ln"], h.val(1))
                d.scalar_tensor_tensor(out=GB[:, :], in0=GB[:, :], scalar=0.0, in1=GT[:, :], op0=ALU.min,
                                       op1=ALU.subtract).then_inc(S["log_gate"], 1)
                d.wait_ge(S["log_gate"], h.val(1))
                d.tensor_tensor_scan(GT[:, :], cst("chunk_reset"), GB[:, :], 0.0, ALU.mult, ALU.add)\
                    .then_inc(S["gate_sums"], 1)
                d.wait_ge(S["gate_sums"], h.val(1))
                b = prompt(GT[:, :]).rearrange("p a (c t) -> p a c t", t=CH)
                d.tensor_tensor(prompt(ED[:, :]).rearrange("p a (c t) -> p a c t", t=CH),
                                b[:, :, :, CH - 1:CH].broadcast_to([P, 2, HPT // CH, CH]), b, ALU.subtract)\
                    .then_inc(S["to_last"], 1)
                b = decode(GT[:, :]).rearrange("p (s t) -> p s t", t=DEC_T)
                d.tensor_tensor(decode(ED[:, :]).rearrange("p (s t) -> p s t", t=DEC_T),
                                b[:, :, DEC_T - 1:DEC_T].broadcast_to([P, DEC_B, DEC_T]), b, ALU.subtract)\
                    .then_inc(S["to_last"], 1)
                d.wait_ge(S["exp_b"], h.val(1))
                d.wait_ge(freed[at("gq")[0].mod(2)], left(at("gq")[0]))
                d.scalar_tensor_tensor(out=GQ[:, :], in0=GQ[:, :], scalar=DK ** -0.5, in1=EB[:, :], op0=ALU.mult,
                                       op1=ALU.mult).then_inc(S["q_decayed"], 1)
                d.wait_ge(S["q_decayed"], h.val(1))
                d.tensor_tensor(QDM[:, :, :], decode(GQ[:, :]).unsqueeze(1).broadcast_to([P, DEC_B, 32]),
                                cst("dec_cols").rearrange("p (b c) -> p b c", b=DEC_B), ALU.mult).then_inc(S["q_by_seq"], 1)
                lo(v + (1 + LEAD))
                v = at("block0")[1]
                for s in range(ADA_V):
                    lo(v + (s + LEAD), HU - POOL_COLS if s < ADA_V - LEAD else HU)
                    if s == 2:
                        d.wait_ge(S["exp_to_last"], h.val(1))
                        d.wait_ge(freed[at("gk")[0].mod(2)], left(at("gk")[0]))
                        d.tensor_tensor(ED[:, :], ED[:, :], GK[:, :], ALU.mult).then_inc(S["k_to_last"], 1)
                m, v = at("gv0")
                d.wait_ge(S["k_to_last"], h.val(1))
                d.wait_ge(S["exp_minus_b"], h.val(1))
                d.tensor_tensor(GK[:, :], GK[:, :], EN[:, :], ALU.mult).then_inc(S["k_decayed"], 1)
                lo(v + LEAD)
                mod_block(m + -1, block_of(0))
                lo(v + (1 + LEAD))
                d.wait_ge(S["k_decayed"], h.val(1))
                d.wait_ge(S["a_mm"], two.val(2))
                d.wait_ge(S["k_by_token"], two.val(2))
                d.tensor_tensor(KDM[:, :, :], KDT[0:32, NB, :].unsqueeze(1).broadcast_to([32, DEC_B, P]),
                                cst("dec_rows")[0:32, :].unsqueeze(2).broadcast_to([32, DEC_B, P]), ALU.mult)\
                    .then_inc(S["k_by_seq"], 1)
                d.copy_predicated(ATT[:, :, :], cst("chunk_mask").bitcast(I32).unsqueeze(1).broadcast_to([P, NB, P]),
                                  PS[:, 2, :].rearrange("p (b t) -> p b t", b=NB)).then_inc(S["a_masked"], 1)
                d.copy_predicated(ATD[:, :], cst("dec_mask")[0:32, :].bitcast(I32), PS[0:32, 3, 0:32])\
                    .then_inc(S["a_masked"], 1)
                v = at("gv1")[1]
                lo(v + LEAD)
                lo(v + (1 + LEAD))
                v = at("block1")[1]
                for s in range(ADA_V):
                    lo(v + (s + LEAD), HU - POOL_COLS if s < ADA_V - LEAD else HU)
                m, v = at("gg0")
                lo(v + LEAD)
                mod_block(m + -1, block_of(1))
                for c in range(GG0_CHUNKS):
                    if c == 8:
                        lo(v + (1 + LEAD))
                    update(c)
                m, v = at("gg1")
                lo(v + LEAD)
                for c in range(GG0_CHUNKS, NCH):
                    update(c)
                for b in range(DEC_B):
                    last = scol(b) + DEC_T - 1
                    d.wait_ge(S["seq_mm"], At(DEC_B * r, i, 2 * DEC_B).val(b + 1))
                    d.scalar_tensor_tensor(out=SD[:, b, :], in0=SD[:, b, :], scalar=EB[:, last:last + 1],
                                           in1=PS[:, 2, 0:DV], op0=ALU.mult, op1=ALU.add)\
                        .then_inc(S["seq_up"], 1)
                    if b == 3:
                        lo(v + (1 + LEAD))
                d.wait_ge(S["norm_rms"], h.val(1))
                d.reciprocal(VR[:, 2, :], VR[:, 1, :]).then_inc(S["norm_r"], 1)
                d.wait_ge(S["norm_r"], h.val(1))
                for b in range(NB // 2, NB):
                    d.tensor_scalar(OT[:, b, :], o_block(b), VR[:, 2, b:b + 1], None, ALU.mult)\
                        .then_inc(S["out_scaled_d"], 1)
                v = at("block2")[1]
                for s in range(ADA_V):
                    lo(v + (s + LEAD), HU - POOL_COLS if s < ADA_V - LEAD else HU)
                    if s != 4:
                        continue
                    d.wait_ge(S["out_turned"], h.val(1))
                    for e in range(2):
                        tile = MIX[:, two.val(8 + e), :]
                        g = HP_AT["g_gla"][0] + e
                        gain = HP[:, g:g + 1]
                        d.wait_ge(freed[at(f"gg{e}")[0].mod(2)], left(at(f"gg{e}")[0]))
                        d.scalar_tensor_tensor(out=prompt(tile), in0=PS[:, e, :].rearrange("p (a n) -> p a n", a=2),
                                               scalar=gain, in1=prompt(GG[e][:, :]), op0=ALU.mult, op1=ALU.mult)
                        d.scalar_tensor_tensor(out=decode(tile), in0=PS[:, 2, 32 * e:32 * e + 32], scalar=gain,
                                               in1=decode(GG[e][:, :]), op0=ALU.mult, op1=ALU.mult)\
                            .then_inc(S["mixed"], 1)

        mod_block(At(M_OUT - 1), At(B_HEAD + 3 * GH - 1))
        scale_by(At(M_OUT - 1), "g_ffn", 4 * KT, KT, 0)
        for k in range(KT):
            d.wait_ge(S["h_hi"], KT + k + 1)
            d.tensor_tensor(HL[:, k, :], MIX[:, k, :], HH[:, k, :].bitcast(F32), ALU.subtract)\
                .then_inc(S["h_lo"], 1)

        def residual(m, k, sec, count):
            tile = X1[:, k, :]
            if count.i is not None or count.base:
                d.wait_ge(S["x1_done"], count.val())
            d.tensor_tensor(SC[:, :].rearrange("p (a n) -> p a n", a=2), bank_decode(banks(m)),
                            MOD[:, KT * sec + k, 1:NSEQ].rearrange("p (a n) -> p a n", a=2),
                            ALU.mult).then_inc(S["x1_tmp"], 1)
            d.scalar_tensor_tensor(out=prompt(tile), in0=bank_prompt(banks(m)), scalar=MOD[:, KT * sec + k, 0:1],
                                   in1=prompt(tile), op0=ALU.mult, op1=ALU.add).then_inc(freed[m.mod(2)], 1)
            d.wait_ge(S["x1_tmp"], count.val(1))
            d.tensor_tensor(decode(tile), decode(tile), SC[:, :], ALU.add).then_inc(S["x1_done"], 1)

        for k in range(KT):
            m, v = At(M_OUT + k), At(V_OUT + 2 * k)
            lo(v + LEAD)
            lo(v + (1 + LEAD))
            if k == 0:
                continue
            d.wait_ge(S["used"], v.val(2))
            if k == 1:
                d.wait_ge(x1_in[0], 16)
                residual(m + -1, 0, 2, At(0))
            if k % 4 == 0:
                d.wait_ge(x1_in[k // 4], 16)
            residual(m, k, 2, At(k))
        for w in range(2):
            d.wait_ge(S["rms"], 2 + w)
            d.reciprocal(RN[:, HT * w:HT * w + HT], RN[:, HT * w:HT * w + HT]).then_inc(S["rstd"], 1)

        def norm_x1(k):
            if k >= 4:
                d.wait_ge(S["h_lo"], 2 * KT + k - 3)
            d.tensor_tensor(TM1[k % 4][:, :], X1[:, k, :], RN[:, :], ALU.mult).then_inc(S["nrm"], 1)

        d.wait_ge(S["rstd"], 4)
        norm_x1(0)
        norm_x1(1)
        for k in range(KT):
            if k + 2 < KT:
                norm_x1(k + 2)
            d.wait_ge(S["h_hi"], 2 * KT + k + 1)
            d.tensor_tensor(HL[:, k, :], TM1[k % 4][:, :], HH[:, k, :].bitcast(F32), ALU.subtract)\
                .then_inc(S["h_lo"], 1)
        with d.Fori(0, NFC) as i:
            for f in range(FC):
                m, v = At(M_FFN + 2 * f + 1, i, M_CHUNK), At(V_FFN + 4 * f, i, V_CHUNK)
                for s in range(4):
                    lo(v + (s + LEAD))
                d.wait_ge(S["used"], v.val(4))
                d.wait_ge(freed[(m + 1).mod(2)], left(m + -1))
                d.tensor_tensor(halves(AF[f % 2][:, :]), halves(SG[f % 2][:, :]), banks(m), ALU.mult)\
                    .then_inc(freed[m.mod(2)], 1)
                d.wait_ge(freed[m.mod(2)], left(m))
                d.wait_ge(S["act_hi"], At(f, i, FC).val(1))
                d.tensor_tensor(AL[:, f, :], AF[f % 2][:, :], AH[:, f, :].bitcast(F32), ALU.subtract)\
                    .then_inc(S["act_lo"], 1)
            for u in range(KT // 2):
                v = At(V_FFN + 4 * FC + u, i, V_CHUNK)
                lo(v + LEAD)
                for c in range(2):
                    k = 2 * u + c
                    if c == 0:
                        d.wait_ge(S["down_a"], At(u, i, KT // 2).val(1))
                    else:
                        d.wait_ge(S["used"], v.val(1))
                    residual(At(M_FFN + 2 * FC + k, i, M_CHUNK), k, 5, At(KT + k, i, KT))
        for w in range(2):
            d.wait_ge(S["rms"], 4 + w)
            d.reciprocal(RN[:, HT * w:HT * w + HT], RN[:, HT * w:HT * w + HT]).then_inc(S["rstd"], 1)
        d.wait_ge(S["rstd"], 6)
        g = PRM["g_final"][0]
        for k in range(KT):
            d.scalar_tensor_tensor(out=X1[:, k, :], in0=X1[:, k, :], scalar=PR[:, g + k:g + k + 1], in1=RN[:, :],
                                   op0=ALU.mult, op1=ALU.mult).then_inc(S["fin"], 1)

    @block.tensor
    def _(e):
        def ada_block(m, v, b, side=None, share=None):
            bank = PJ[:, 2 * m.mod(2), :]
            if m.i is not None or m.base >= 2:
                e.wait_ge(freed[m.mod(2)], left(m, 0))
            for s in range(ADA_V):
                e.wait_ge(S["lo"], v.val(s + 1))
                if share and s in share:
                    e.wait_ge(S["lo_pool"], share[s])
                wh, wl = WH[(v + s).mod(HIS)], WL[(v + s).mod(RAW)]
                for c in range(2):
                    k = 2 * s + c
                    rows = CS[:, CPITCH * k:CPITCH * k + P]
                    e.matmul(bank, rows, wh[:, 512 * c:512 * c + 512], start=(k == 0), stop=False)
                    mm = e.matmul(bank, rows, wl[:, 512 * c:512 * c + 512], start=False, stop=(k == KT - 1))
                mm.then_inc(S["used"], 1)
                for job in (side or {}).get(s, ()):
                    job()

        def turn_rows(m, b):
            e.wait_ge(S["ada_rows"], b.val(1))
            lo, up = CST["sel"]
            for f in range(4):
                mm = e.matmul(PJ[:, 2 * m.mod(2) + 1, NSEQ * f:NSEQ * f + NSEQ], ADAR[:, P * f:P * f + P],
                              CN[0:64, lo:up], start=True, stop=True)
            mm.then_inc(S["ada_t"], 1)

        def sum_squares(*parts):
            for w in range(2):
                for n, x in enumerate(parts):
                    mm = e.matmul(PS[:, w, 0:HT], ones, x[:, HT * w:HT * w + HT], start=(n == 0),
                                  stop=(n == len(parts) - 1))
                if w or len(parts) > 1:
                    mm.then_inc(S["sum_done"], 1)

        def accumulate(m, v, k):
            out = [PJ[:, 2 * m.mod(2) + w, 0:HT] for w in range(2)]
            wh, wl = (t[:, P * (k % 8):P * (k % 8) + P] for t in (WH[v.mod(HIS)], WL[v.mod(RAW)]))
            for n, (x, y) in enumerate(((wh, HH), (wh, HL), (wl, HH))):
                for w in range(2):
                    mm = e.matmul(out[w], x, y[:, k, HT * w:HT * w + HT], start=(k == 0 and n == 0),
                                  stop=(k == KT - 1 and n == 2))
            if k % 8 == 7:
                mm.then_inc(S["used"], 1)

        def project(m, v, side=None, ready=None):
            e.wait_ge(freed[m.mod(2)], left(m, 0))
            for k in range(KT):
                if k % 8 == 0:
                    e.wait_ge(S["lo"], v.val(k // 8 + 1))
                if ready is not None:
                    e.wait_ge(S["h_lo"], ready + k + 1)
                accumulate(m, v + k // 8, k)
                for job in (side or {}).get(k, ()):
                    job()

        def project_two(m, v, ready):
            for t in range(2):
                e.wait_ge(freed[(m + t).mod(2)], left(m + t, 0))
            for k in range(KT):
                if k % 8 == 0:
                    e.wait_ge(S["lo"], v.val(k // 4 + 2))
                e.wait_ge(S["h_lo"], ready + k + 1)
                for t in range(2):
                    accumulate(m + t, v + (k // 8 * 2 + t), k)

        e.wait_ge(S["cs_lo"], 1)

        def sum_x():
            e.wait_ge(S["acc"], KT - 1)
            sum_squares(AC0)

        for b in range(8):
            side = {}
            if b:
                side[3] = [lambda b=b: turn_rows(At(b - 1), At(b - 1))]
            if b == SUM_AT // ADA_V:
                side[SUM_AT % ADA_V] = side.get(SUM_AT % ADA_V, []) + [sum_x]
            shared = [v for v in SHARED if v // ADA_V == b]
            ada_block(At(b), At(ADA_V * b), At(b), side, shared and {v % ADA_V: v - SHARED[0] + 1 for v in shared})
        turn_rows(At(7), At(7))

        def v_by_token():
            e.wait_ge(freed[W_M["v"] % 2], left(At(W_M["v"])))
            e.wait_ge(S["rms"], 1)
            for b in range(NB):
                mm = e.transpose(PS[:, 0, WIN * b:WIN * b + WIN], VTT[:, pcol(b):pcol(b) + WIN], ident)
            mm.then_inc(S["v_t"], 1)
            e.transpose(PS[0:32, 1, 0:P], decode(VTT[:, :]), ident).then_inc(S["v_t"], 1)

        def dec_scores():
            e.wait_ge(S["dec_q_packed"], 2)
            e.wait_ge(S["cache_in"], 96)
            e.wait_ge(S["v_tok"], 2)
            for kv in range(KVH):
                rows = slice(HD * kv, HD * kv + HD)
                for b in range(DEC_B):
                    out = PS[32 * (b % 4):32 * (b % 4) + 32, kv, 160 * (b // 4):160 * (b // 4) + 160]
                    e.matmul(out[:, 0:WIN], QS[rows, b, :], KC[rows, b, :], start=True, stop=True)
                    mm = e.matmul(out[:, WIN:160], QS[rows, b, :], decode(KTT[rows, :]), start=True, stop=True)
                mm.then_inc(S["dec_scores"], 1)

        def dec_turn():
            e.wait_ge(S["dec_probs"], 1)
            for n in range(4):
                mm = e.transpose(PS[:, 2, P * n:P * n + P], LS[:, n // 2, n % 2, 0:WIN], ident)
            mm.then_inc(S["dec_turned"], 1)
            for n in range(4):
                mm = e.transpose(PS[0:32, 3, P * n:P * n + P], LS[:, n // 2, n % 2, WIN:160], ident)
            mm.then_inc(S["dec_turned"], 1)

        def dec_values():
            e.wait_ge(S["dec_by_key"], 2)
            for kv in range(KVH):
                rows = slice(HD * kv, HD * kv + HD)
                for b in range(DEC_B):
                    n, r = 2 * kv + b // 4, 32 * (b % 4)
                    out = PS[rows, 0, 16 * b:16 * b + 16]
                    e.matmul(out, VC[:, b, rows], PT[0][:, n, r:r + 16], start=True, stop=False)
                    mm = e.matmul(out, VTK[0:32, NB, rows], PTN[:, n, r:r + 16], start=False, stop=True)
            mm.then_inc(S["dec_values"], 1)

        project_two(At(M_W), At(V_W), 0)
        jobs = {"q0": {4: [v_by_token]},
                "q2": {3: [lambda: turn_rows(At(W_M["block0"]), At(B_W))]},
                "ga": {2: [lambda: turn_rows(At(W_M["block1"]), At(B_W + 1))], 4: [dec_scores],
                       10: [dec_turn], 13: [dec_values]}}
        for name in W_TILES[2:]:
            if name[0] == "b":
                ada_block(At(W_M[name]), At(W_V[name]), At(B_W + int(name[5])))
            else:
                project(At(W_M[name]), At(W_V[name]), jobs.get(name))
        m, v = At(M_U), At(V_U)

        def scores(q, n):
            job, kv, pair = 4 * q + n, n % 2, n // 2
            rows = slice(HD * kv, HD * kv + HD)
            if job >= 2:
                e.wait_ge(S["att_logits"], job - 1)
            else:
                e.wait_ge(S["dec_stored"], 2)
            for j in range(2):
                for kb in range(1 if q == 0 else 0, 2):
                    keys = pcol(q - 1 + kb)
                    at = 256 * j + WIN * kb
                    mm = e.matmul(PS[:, n % 2, at:at + WIN], MIX[rows, 2 * pair + j, pcol(q):pcol(q) + WIN],
                                  KTT[rows, keys:keys + WIN], start=True, stop=True)
            mm.then_inc(S["att_scores"], 1)

        def turn(q, n):
            job = 4 * q + n
            e.wait_ge(S["att_probs"], 2 * job + 2)
            if job:
                e.wait_ge(S["att_by_key"], job)
            for j in range(2):
                for kb in range(1 if q == 0 else 0, 2):
                    at = 256 * j + WIN * kb
                    mm = e.transpose(PS[:, 2, at:at + WIN], LG[n][:, j, WIN * kb:WIN * kb + WIN], ident)
            mm.then_inc(S["att_turned"], 1)

        def values(q, n):
            job, kv, pair = 4 * q + n, n % 2, n // 2
            rows = slice(HD * kv, HD * kv + HD)
            k0 = 1 if q == 0 else 0
            e.wait_ge(S["att_by_key"], job + 1)
            if n == 0 and q:
                e.wait_ge(S["att_stored"], q)
            for j in range(2):
                for kb in range(k0, 2):
                    mm = e.matmul(PS[rows, 3, WIN * (2 * pair + j):WIN * (2 * pair + j) + WIN], VTK[:, q - 1 + kb, rows],
                                  PT[n % 2][:, 2 * j + kb, :], start=(kb == k0), stop=(kb == 1))
            mm.then_inc(S["att_values"], 1)

        for q in range(4):
            side = {}
            for n in range(4):
                for job, k in ((scores, (0, 1, 3, 5)[n]), (turn, (8, 10, 12, 14)[n]), (values, (10, 12, 14, 15)[n])):
                    side.setdefault(k, []).append(lambda job=job, q=q, n=n: job(q, n))
            if q == 2:
                side.setdefault(2, []).append(lambda m=m: turn_rows(m + -1, At(B_U)))
            project(m, v, side)
            m, v = m + 1, v + 2
            if q % 2:
                ada_block(m, v, At(B_U + q // 2))
                m, v = m + 1, v + ADA_V

        with e.Fori(0, GH // 2) as i:
            for r in range(2):
                h, two, four = At(r, i, 2), At(2 * r, i, 4), At(4 * r, i, 8)
                chunks, seqs = At(NCH * r, i, 2 * NCH), At(DEC_B * r, i, 2 * DEC_B)

                def at(name):
                    return (At(M_HEAD + M_HEAD_STEP * r + HEAD_M[name], i, 2 * M_HEAD_STEP),
                            At(V_HEAD + V_HEAD_STEP * r + HEAD_V[name], i, 2 * V_HEAD_STEP))

                def block_of(n):
                    return At(B_HEAD + 3 * r + n, i, 6)

                def share_of(n):
                    before = At(len(SHARED) + (ADA_V - LEAD) * (3 * r + n), i, (ADA_V - LEAD) * 6)
                    return {s: before.val(s - LEAD + 1) for s in range(LEAD, ADA_V)}

                def turn_of(name, n):
                    return lambda: turn_rows(at(name)[0] + -1, block_of(n))

                def gates():
                    e.wait_ge(S["head_in"], At(16 * r, i, 32).val(16))
                    lo, up = HP_AT["w_a2"]
                    for w in range(2):
                        mm = e.matmul(PS[:, w, 0:HT], HP[0:RANK, lo:up], GA[0:RANK, HT * w:HT * w + HT],
                                      start=True, stop=True)
                    mm.then_inc(S["gate_mm"], 1)

                def pool_group():
                    lo, up = HP_AT["w_pool"]
                    for w in range(2):
                        mm = e.matmul(PS[:, 2 + w, 0:HT], HP[:, lo:up], MIX[:, h.val(4), HT * w:HT * w + HT],
                                      start=True, stop=True)
                    mm.then_inc(S["pool_mm"], 1)

                def k_by_token():
                    e.wait_ge(S["k_to_last"], h.val(1))
                    for b in range(NB):
                        mm = e.transpose(PS[:, 0, P * b:P * b + P], ED[:, pcol(b):pcol(b) + P], ident)
                    mm.then_inc(S["k_turned"], 1)
                    e.transpose(PS[0:32, 1, 0:P], decode(ED[:, :]), ident).then_inc(S["k_turned"], 1)

                def inside():
                    e.wait_ge(S["q_decayed"], h.val(1))
                    e.wait_ge(S["k_decayed"], h.val(1))
                    e.wait_ge(S["pool_done"], h.val(1))
                    for b in range(NB):
                        mm = e.matmul(PS[:, 2, P * b:P * b + P], GK[:, pcol(b):pcol(b) + P], GQ[:, pcol(b):pcol(b) + P],
                                      start=True, stop=True)
                    mm.then_inc(S["a_mm"], 1)
                    e.matmul(PS[0:32, 3, 0:32], decode(GK[:, :]), decode(GQ[:, :]), start=True, stop=True)\
                        .then_inc(S["a_mm"], 1)

                def v_turn(x):
                    m = at(f"gv{x}")[0]
                    e.wait_ge(freed[m.mod(2)], left(m))
                    if x == 0:
                        e.wait_ge(S["k_by_token"], two.val(2))
                    else:
                        e.wait_ge(S["gv_by_token"], four.val(2))
                    for b in range(NB):
                        mm = e.transpose(PS[:, 0, P * b:P * b + P], GV[x][:, pcol(b):pcol(b) + P], ident)
                    mm.then_inc(S["gv_turned"], 1)
                    e.transpose(PS[0:32, 1, 0:P], decode(GV[x][:, :]), ident).then_inc(S["gv_turned"], 1)

                def chunk(c):
                    b, rows = c // 4, slice(CH * (c % 4), CH * (c % 4) + CH)
                    if c == 0:
                        e.wait_ge(S["gv_by_token"], four.val(4))
                        e.wait_ge(S["a_masked"], two.val(2))
                    elif c == 1:
                        pass
                    else:
                        e.wait_ge(S["state_up"], chunks.val(c - 1))
                    e.matmul(PS[:, 2 + c % 2, 0:DV], KDT[rows, b, :], GVT[rows, b, :], start=True, stop=True)\
                        .then_inc(S["chunk_mm"], 1)
                    if c % 4 == 0:
                        e.matmul(o_block(b), ATT[:, b, :], GVT[:, b, :], start=True, stop=False, skip_group_check=True)
                    if c:
                        e.wait_ge(S["state_up"], chunks.val(c))
                        at = pcol(c, CH)
                        mm = e.matmul(o_block(b)[rows, :], GQ[:, at:at + CH], SS[c % 2][:, :],
                                      start=False, stop=True, skip_group_check=True)
                    if c == NCH - 1:
                        mm.then_inc(S["out_mm"], 1)

                def sequence(b):
                    out = PS[0:32, 3, 0:DV]
                    if b == 0:
                        e.wait_ge(S["state_up"], chunks.val(NCH))
                        e.wait_ge(S["state_in"], At(16 * r, i, 32).val(16))
                        e.wait_ge(S["k_by_seq"], h.val(1))
                        e.wait_ge(S["q_by_seq"], h.val(1))
                    mm = e.matmul(out, QDM[:, b, :], SD[:, b, :], start=(b == 0), stop=(b == DEC_B - 1))
                    if b == 0:
                        e.matmul(out, ATD[:, :], GVT[0:32, NB, :], start=False, stop=False)
                    if b == DEC_B - 1:
                        mm.then_inc(S["dec_out_mm"], 1)
                    if b:
                        e.wait_ge(S["seq_up"], seqs.val(b))
                    e.matmul(PS[:, 2, 0:DV], KDM[:, b, :], GVT[0:32, NB, :], start=True, stop=True)\
                        .then_inc(S["seq_mm"], 1)

                def o_turn():
                    e.wait_ge(S["out_scaled_a"], At(3 * r, i, 6).val(3))
                    e.wait_ge(S["out_scaled_d"], two.val(2))
                    e.wait_ge(S["seq_up"], seqs.val(DEC_B))
                    for x in range(2):
                        for b in range(NB):
                            e.transpose(PS[:, x, P * b:P * b + P], OT[:, b, P * x:P * x + P], ident)
                        mm = e.transpose(PS[:, 2, 32 * x:32 * x + 32], OTD[:, P * x:P * x + P], ident[0:32, 0:32])
                    mm.then_inc(S["out_turned"], 1)

                def spread(k, f, ns):
                    return {k + j: [lambda c=c: f(c)] for j, c in enumerate(ns)}

                project(*at("gq"), {3: [turn_of("gq", -1)]})
                project(*at("gk"), {2: [gates], 5: [pool_group]})
                ada_block(*at("block0"), block_of(0), share=share_of(0))
                project(*at("gv0"), {2: [k_by_token], 3: [turn_of("gv0", 0)], 5: [inside]})
                project(*at("gv1"), {2: [lambda: v_turn(0)]})
                ada_block(*at("block1"), block_of(1), {2: [lambda: v_turn(1)]}, share_of(1))
                project(*at("gg0"), {2: [turn_of("gg0", 1)], **spread(3, chunk, range(GG0_CHUNKS))})
                project(*at("gg1"), {**spread(0, chunk, range(GG0_CHUNKS, NCH)),
                                     **spread(NCH - GG0_CHUNKS + 1, sequence, range(DEC_B))})
                ada_block(*at("block2"), block_of(2), {3: [o_turn]}, share_of(2))

        turn_rows(At(M_OUT - 1), At(B_HEAD + 3 * GH - 1))
        project_two(At(M_OUT), At(V_OUT), KT)
        for k in range(2, KT):
            project(At(M_OUT + k), At(V_OUT + 2 * k))
        e.wait_ge(S["x1_acc"], KT)
        e.wait_ge(S["x1_sq"], KT)
        sum_squares(AC, QX[1])
        def chunk(c0, i=None, n=0):
            for f in range(FC):
                m = At(M_FFN + M_CHUNK * c0 + 2 * f, i, n * M_CHUNK)
                v = At(V_FFN + V_CHUNK * c0 + 4 * f, i, n * V_CHUNK)
                made = i is not None or f > 0
                first = [(t, k) for t in range(2) for k in range(KT // 2)]
                second = [(t, k) for t in (2, 3) for k in range(KT // 2, KT)]
                for t, k in (first if made else sorted(first, key=lambda x: x[1])) + second:
                    if k == 0:
                        e.wait_ge(freed[(m + t).mod(2)], left(m + t, 0))
                    if k % (KT // 2) == 0:
                        e.wait_ge(S["lo"], v.val(t + 1))
                    if not made:
                        e.wait_ge(S["h_lo"], 2 * KT + k + 1)
                    accumulate(m + t % 2, v + t, k)
            for u in range(KT // 2):
                v = At(V_FFN + V_CHUNK * c0 + 4 * FC + u, i, n * V_CHUNK)
                m = [At(M_FFN + M_CHUNK * c0 + 2 * FC + 2 * u + c, i, n * M_CHUNK) for c in range(2)]
                e.wait_ge(S["lo"], v.val(1))
                order = [(k + x, c) for k in range(0, FC, 2) for c in range(2) for x in range(2)] if u == 0 else \
                    [(k, c) for c in range(2) for k in range(FC)]
                for k, c in order:
                    if k == 0:
                        e.wait_ge(freed[m[c].mod(2)], left(m[c], 0))
                    if u == 0 and c == 0:
                        e.wait_ge(S["act_lo"], At(FC * c0 + k, i, n * FC).val(1))
                    w0 = P * (FC * c + k)
                    wh, wl = WH[v.mod(HIS)][:, w0:w0 + P], WL[v.mod(RAW)][:, w0:w0 + P]
                    for x, (w, y) in enumerate(((wh, AH), (wh, AL), (wl, AH))):
                        for a in range(2):
                            mm = e.matmul(PJ[:, 2 * m[c].mod(2) + a, 0:HT], w, y[:, k, HT * a:HT * a + HT],
                                          start=(k == 0 and x == 0), stop=(k == FC - 1 and x == 2))
                    if k == FC - 1:
                        mm.then_inc(S["used" if c else "down_a"], 1)

        chunk(0)
        with e.Fori(0, NFC // 2) as i:
            chunk(1, i, 2)
            chunk(2, i, 2)
        e.wait_ge(S["x1_acc"], 2 * KT)
        e.wait_ge(S["x1_sq"], 2 * KT)
        sum_squares(AC, QX[1])


def t5_buckets():
    n = np.arange(WIN)
    nf = np.maximum(n, 16).astype(np.float32)
    large = 16 + (np.log(nf / np.float32(16)) / np.float32(np.log(8.0)) * 16).astype(np.int32)
    return np.where(n < 16, n, np.minimum(large, 31))


def by_feature(prompt_rows, decode_rows):
    x = np.concatenate([prompt_rows[0:HPT], decode_rows, prompt_rows[HPT:]], 0)
    return np.ascontiguousarray(x.reshape(NT, -1, P).transpose(2, 1, 0))


def by_token(x):
    x = x.transpose(2, 1, 0).reshape(NT, -1)
    return np.concatenate([x[0:HPT], x[HPT + 2 * HST:]], 0), x[HPT:HPT + 2 * HST]


def vectors(*xs):
    return np.concatenate([np.asarray(x).reshape(-1, P).T for x in xs], 1)


def weight_stream(w_ada, w_in, w_out, w_gu, w_down):
    out = np.zeros((V_ALL, P, HU), np.float32)

    def tiles(v, w):
        n = w.shape[1] // P
        x = w.reshape(2, 8, P, n, P).transpose(3, 0, 2, 1, 4)
        out[v:v + 2 * n] = x.reshape(2 * n, P, HU)

    def pairs(v, w):
        n = w.shape[1] // (2 * P)
        x = w.reshape(2, 8, P, n, 2, P).transpose(3, 0, 4, 2, 1, 5)
        out[v:v + 4 * n] = x.reshape(4 * n, P, HU)

    def ada(v, w):
        n = w.shape[1] // 512
        out[v:v + 8 * n] = w.reshape(8, 2, P, n, 512).transpose(3, 0, 2, 1, 4).reshape(8 * n, P, HU)

    ada(0, w_ada[:, 0:8 * 512])
    places = [W_V["block0"], W_V["block1"]] + [V_U + n * V_U_STEP + 4 for n in range(2)]
    places += [V_HEAD + h * V_HEAD_STEP + HEAD_V[f"block{n}"] for h in range(GH) for n in range(3)]
    for b, v in enumerate(places):
        ada(v, w_ada[:, 512 * (8 + b):512 * (9 + b)])
    at = np.cumsum([0, 512, 128, 128, 512, 512, 512, 1024, 1024, RANK])
    q, k_, v_, u, gq, gk, gv, gg, ga = (w_in[:, at[n]:at[n + 1]] for n in range(9))
    ga = np.concatenate([ga, np.zeros((D, P - RANK), np.float32)], 1)
    q = q.reshape(D, KVH, GRP, HD).transpose(0, 2, 1, 3).reshape(D, 512)
    pairs(V_W, np.concatenate([k_, v_], 1))
    tiles(W_V["q0"], q[:, 0:2 * P])
    tiles(W_V["q2"], q[:, 2 * P:])
    tiles(W_V["ga"], ga)
    for n in range(2):
        tiles(V_U + V_U_STEP * n, u[:, 2 * P * n:2 * P * (n + 1)])
    for h in range(GH):
        for n, w in (("gq", gq[:, P * h:P * h + P]), ("gk", gk[:, P * h:P * h + P]), ("gv0", gv[:, DV * h:DV * h + DV]),
                     ("gg0", gg[:, DV * h:DV * h + DV])):
            tiles(V_HEAD + V_HEAD_STEP * h + HEAD_V[n], w)
    wo = np.concatenate([w_out[0:512].reshape(KVH, GRP, HD, D).transpose(1, 0, 2, 3).reshape(512, D), w_out[512:]], 0)
    pairs(V_OUT, wo[:, 0:2 * P])
    tiles(V_OUT + 4, wo[:, 2 * P:])
    for c in range(NFC):
        v = V_FFN + V_CHUNK * c
        for f in range(FC):
            n = P * (FC * c + f)
            pairs(v + 4 * f, np.concatenate([w_gu[:, n:n + P], w_gu[:, DFF + n:DFF + n + P]], 1))
        w = w_down[P * FC * c:P * FC * (c + 1)].reshape(FC, P, KT // 2, 2, P)
        out[v + 4 * FC:v + V_CHUNK] = w.transpose(2, 1, 3, 0, 4).reshape(KT // 2, P, HU)
    return out


def constants():
    c = np.zeros((P, CST_N), np.float32)

    def put(name, x):
        a, b = CST[name]
        c[0:x.shape[0], a:b] = x

    put("ident", np.eye(P, dtype=np.float32))
    put("ones", np.ones((P, P), np.float32))
    sel = np.zeros((64, NSEQ), np.float32)
    for base in (0, LO_AT):
        sel[base, 0] = 1
        for s in range(DEC_B * DEC_T):
            sel[base + 1 + s // DEC_T, 1 + s] = 1
    put("sel", sel)
    reset = np.ones((P, NT), np.float32)
    for b in range(NCH):
        reset[:, pcol(b, CH)] = 0
    for b in range(DEC_B):
        reset[:, scol(b)] = 0
    put("chunk_reset", reset)
    s = np.arange(P)
    put("chunk_mask", ((s[:, None] // CH == s[None] // CH) & (s[:, None] <= s[None])).astype(np.float32))
    s = np.arange(32)
    put("dec_mask", ((s[:, None] // DEC_T == s[None] // DEC_T) & (s[:, None] <= s[None])).astype(np.float32))
    put("dec_rows", (s[:, None] // DEC_T == np.arange(DEC_B)[None]).astype(np.float32))
    inv = [[1.0 / min(2 << q, t + 1) for t in range(16)] for q in range(4)]
    put("dec_cols", np.tile((np.arange(DEC_B)[:, None] == s[None] // DEC_T).astype(np.float32).reshape(1, -1), (P, 1)))
    put("pool_inv", np.tile(np.array(inv, np.float32).reshape(1, 64), (P, 1)))
    put("eps", np.full((P, 1), EPS, np.float32))
    m = np.zeros((P, MSK_N), np.float32)
    dist = WIN + np.arange(P)[:, None] - np.arange(256)[None]
    keep = (dist >= 0) & (dist < WIN)
    m[:, MSK["keep"][0]:MSK["keep"][1]] = keep
    m[:, MSK["neg"][0]:MSK["neg"][1]] = np.where(keep, 0.0, NEG)
    row = np.arange(P)
    bq, t = row // 32, row % 32 // GRP % DEC_T
    keep = np.zeros((P, 2, 160), bool)
    past, new = np.arange(WIN), np.arange(32)
    for g in range(2):
        keep[:, g, 0:WIN] = past[None] > t[:, None]
        keep[:, g, WIN:] = (new[None] // DEC_T == (4 * g + bq)[:, None]) & (new[None] % DEC_T <= t[:, None])
    keep = keep.reshape(P, 320)
    m[:, MSK["keep_dec"][0]:MSK["keep_dec"][1]] = keep
    m[:, MSK["neg_dec"][0]:MSK["neg_dec"][1]] = np.where(keep, 0.0, NEG)
    return c, m


def biases(rel_bias):
    table = rel_bias[t5_buckets()].T
    dist = np.clip(WIN + np.arange(P)[:, None] - np.arange(256)[None], 0, WIN - 1)
    full = np.ascontiguousarray(table[:, dist].transpose(1, 0, 2))
    row = np.arange(P)
    j, t = row % GRP, row % 32 // GRP % DEC_T
    key = np.concatenate([np.arange(WIN) - WIN, np.arange(32) % DEC_T])
    dist = np.clip(t[:, None] - key[None], 0, WIN - 1)
    dec = np.stack([table[(GRP * kv + j)[:, None], dist] for kv in range(KVH)], 1)
    return full, np.ascontiguousarray(np.repeat(dec[:, :, None], 2, 2))


def kernel(x_prompt, x_sample, cache_win_k, cache_win_v, state_pool, state_gla, c_prompt, c_sample,
           w_ada, b_ada, g_mix, g_ffn, w_in, w_out, rel_bias, sinks, w_pool, pool_scale,
           w_a2, b_a2, g_gla, w_gu, w_down, g_final):
    import concourse.bacc as bacc
    from concourse.bass_utils import run_bass_kernel_spmd

    consts, masks = constants()
    row = np.arange(P)
    sinks_dec = np.stack([sinks[0][GRP * kv + row % GRP] for kv in (0, 0, 1, 1)], 1)
    c = np.concatenate([c_prompt, c_sample], 0).reshape(9, KT, P).transpose(2, 1, 0).reshape(P, KT * 9)
    params = np.concatenate([vectors(g_mix[0], g_ffn[0], g_final, b_ada[0]), np.tile(sinks[0][None], (P, 1)),
                             sinks_dec, c], 1)
    head_params = np.zeros((GH, P, HP_N), np.float32)
    for h in range(GH):
        hp = head_params[h]
        hp[:, 0:P] = w_pool[0, h]
        hp[0:RANK, P:2 * P] = w_a2[0][:, P * h:P * h + P]
        hp[:, 2 * P:] = vectors(b_a2[0][P * h:P * h + P], g_gla[0][DV * h:DV * h + DV], pool_scale[0][P * h:P * h + P])
    bias, bias_dec = biases(np.asarray(rel_bias))
    arrays = {
        "weights": weight_stream(*(np.asarray(w[0]) for w in (w_ada, w_in, w_out, w_gu, w_down))),
        "xT": by_feature(np.asarray(x_prompt[0]), np.asarray(x_sample).reshape(DEC_B * DEC_T, D)),
        "params": params, "consts": consts, "masks": masks, "bias": bias, "bias_dec": bias_dec,
        "head_params": head_params,
        "k_cache": np.asarray(cache_win_k[0]).reshape(DEC_B, WIN, P).transpose(2, 0, 1),
        "v_cache": np.asarray(cache_win_v[0]).reshape(DEC_B, WIN, P).transpose(1, 0, 2),
        "pool_state": np.asarray(state_pool[0]).reshape(DEC_B, BUF, 4, P).transpose(3, 2, 0, 1),
        "gla_state": np.asarray(state_gla[0]).transpose(1, 2, 0, 3),
    }
    arrays = {n: np.ascontiguousarray(x) for n, x in arrays.items()}
    shapes = {
        "yT": (P, KT, NT), "kv_prompt": (2, P, WIN), "kv_dec": (2, P, DEC_B * DEC_T), "k_past": (P, DEC_B, WIN - DEC_T),
        "v_past": (WIN - DEC_T, DEC_B, P), "pool_prompt": (P, 4, BUF), "pool_dec": (P, 4, DEC_B, BUF),
        "gla_prompt": (GH, P, DV), "gla_dec": (GH, P, DEC_B, DV),
    }
    nc = bacc.Bacc("TRN2", target_bir_lowering=False, num_devices=1, dynamic_dma_scratch_size=4096)
    ins = {n: nc.dram_tensor(f"in_{n}", x.shape, F32, kind="ExternalInput").ap() for n, x in arrays.items()}
    outs = {n: nc.dram_tensor(f"out_{n}", s, F32, kind="ExternalOutput").ap() for n, s in shapes.items()}
    build(nc, ins, outs)
    res = run_bass_kernel_spmd(nc, [{f"in_{n}": x for n, x in arrays.items()}], core_ids=[0]).results[0]
    o = {n: res[f"out_{n}"] for n in shapes}

    y, y_dec = by_token(o["yT"])
    kv_shape = (DEC_B, WIN, KVH, HD)
    kp, vp = (np.ascontiguousarray(x.T).reshape(1, 1, WIN, KVH, HD) for x in o["kv_prompt"])
    new_k, new_v = (x.reshape(P, DEC_B, DEC_T).transpose(1, 2, 0) for x in o["kv_dec"])
    k_dec = np.concatenate([o["k_past"].transpose(1, 2, 0), new_k], 1).reshape(1, *kv_shape)
    v_dec = np.concatenate([o["v_past"].transpose(1, 0, 2), new_v], 1).reshape(1, *kv_shape)
    pp = o["pool_prompt"].transpose(2, 1, 0).reshape(1, 1, BUF, 512)
    pd = o["pool_dec"].transpose(2, 3, 1, 0).reshape(1, DEC_B, BUF, 512)
    return (y[None], y_dec.reshape(DEC_B, DEC_T, D), kp, vp, pp, o["gla_prompt"][None, None],
            k_dec, v_dec, pd, o["gla_dec"].transpose(2, 0, 1, 3)[None])
```
